# Optimizing a Trainium2 kernel written in Bass

```python
import math
import jax, jax.numpy as jnp
from jax import lax
import numpy as np

D_MODEL = 1024
BATCH = 1
SEQ = 1024
DEPTH = 1

GRID_W = 64
CTX_LEN = 256

H_A = 8
KV_A = 2
G_A = H_A // KV_A
DH_A = 64
WINDOW = 128
BLOCK = 128
BAND = BLOCK + 2 * WINDOW

H_B = 8
NOPE_B = 64
ROPE_B = 32
V_B = 64
Q_RANK = 384
KV_RANK = 256
MLA_SCALE = (NOPE_B + ROPE_B) ** -0.5

W_QA = H_A * DH_A
W_KA = KV_A * DH_A
W_VA = KV_A * DH_A
IN_WIDTHS = (W_QA, W_KA, W_VA, Q_RANK, KV_RANK, ROPE_B)
IN_DIM = sum(IN_WIDTHS)
SPLIT_POINTS = tuple(int(v) for v in np.cumsum(IN_WIDTHS)[:-1])
MIX_DIM = H_A * DH_A + H_B * V_B

N_EXPERTS = 16
CAP_FACTOR = 2
D_FF = 512

ROPE_BASE = 10000.0
EPS = 1e-6


def rmsnorm(x, w):
    xf = x.astype(jnp.float32)
    y = xf * lax.rsqrt(jnp.mean(xf * xf, axis=-1, keepdims=True) + EPS)
    return (y * w.astype(jnp.float32)).astype(x.dtype)

def modulate(h, shift, scale):
    return h * (1 + scale) + shift

def axial_rope(x, rows, cols):
    d = x.shape[-1]
    da = d // 2
    nf = da // 2
    inv = ROPE_BASE ** (-jnp.arange(nf, dtype=jnp.float32) / nf)

    def rot(xa, pos):
        ang = pos.astype(jnp.float32)[:, None] * inv[None, :]
        cos = jnp.cos(ang)[None, :, None, :]
        sin = jnp.sin(ang)[None, :, None, :]
        x1, x2 = xa[..., :nf], xa[..., nf:]
        return jnp.concatenate([x1 * cos - x2 * sin, x1 * sin + x2 * cos], axis=-1)

    xf = x.astype(jnp.float32)
    out = jnp.concatenate([rot(xf[..., :da], rows), rot(xf[..., da:], cols)], axis=-1)
    return out.astype(x.dtype)

def gqa_sink_attend(qb, keys, vals, bias, sink_g):
    s = jnp.einsum('bqkgd,bskd->bkgqs', qb, keys, preferred_element_type=jnp.float32) * (DH_A ** -0.5)
    if bias is not None:
        s = s + bias
    b, q = qb.shape[0], qb.shape[1]
    s_sink = jnp.broadcast_to(sink_g.astype(jnp.float32)[None, :, :, None, None], (b, KV_A, G_A, q, 1))
    p = jax.nn.softmax(jnp.concatenate([s, s_sink], axis=-1), axis=-1)[..., :-1]
    o = jnp.einsum('bkgqs,bskd->bqkgd', p.astype(vals.dtype), vals)
    return o.reshape(b, q, H_A * DH_A)

def window_attention_latent(q, k, v, kc, vc, sink_g):
    b, s_len = q.shape[:2]
    lc = kc.shape[1]
    nb = s_len // BLOCK
    qg = q.reshape(b, s_len, KV_A, G_A, DH_A)
    pad = ((0, 0), (WINDOW, WINDOW), (0, 0), (0, 0))
    kp = jnp.pad(k, pad)
    vp = jnp.pad(v, pad)
    ctx_bias = jnp.zeros((BLOCK, lc), jnp.float32)

    def block(i):
        start = i * BLOCK
        qb = lax.dynamic_slice_in_dim(qg, start, BLOCK, axis=1)
        kb = lax.dynamic_slice_in_dim(kp, start, BAND, axis=1)
        vb = lax.dynamic_slice_in_dim(vp, start, BAND, axis=1)
        tq = start + jnp.arange(BLOCK)
        ts = start - WINDOW + jnp.arange(BAND)
        valid = (jnp.abs(tq[:, None] - ts[None, :]) <= WINDOW) & (ts[None, :] >= 0) & (ts[None, :] < s_len)
        band_bias = jnp.where(valid, 0.0, -jnp.inf).astype(jnp.float32)
        keys = jnp.concatenate([kc, kb], axis=1)
        vals = jnp.concatenate([vc, vb], axis=1)
        bias = jnp.concatenate([ctx_bias, band_bias], axis=1)
        return gqa_sink_attend(qb, keys, vals, bias, sink_g)

    out = lax.map(block, jnp.arange(nb))
    return jnp.transpose(out, (1, 0, 2, 3)).reshape(b, s_len, H_A * DH_A)

def mla_attend(qn, qr, kn, kr, v):
    s = (jnp.einsum('bqhd,bkhd->bhqk', qn, kn, preferred_element_type=jnp.float32)
         + jnp.einsum('bqhr,bkr->bhqk', qr, kr, preferred_element_type=jnp.float32)) * MLA_SCALE
    p = jax.nn.softmax(s, axis=-1)
    o = jnp.einsum('bhqk,bkhd->bqhd', p.astype(v.dtype), v)
    return o.reshape(qn.shape[0], qn.shape[1], H_B * V_B)

def mla_latent(qn, qr, kn, kr, v):
    b, s_len = qn.shape[:2]
    nb = s_len // BLOCK

    def block(i):
        start = i * BLOCK
        qnb = lax.dynamic_slice_in_dim(qn, start, BLOCK, axis=1)
        qrb = lax.dynamic_slice_in_dim(qr, start, BLOCK, axis=1)
        return mla_attend(qnb, qrb, kn, kr, v)

    out = lax.map(block, jnp.arange(nb))
    return jnp.transpose(out, (1, 0, 2, 3)).reshape(b, s_len, H_B * V_B)

def project_groups(t, w_in, q_norm, kv_norm, w_q_up, w_kv_up):
    bt, n = t.shape[:2]
    p = jnp.einsum('bsd,de->bse', t, w_in)
    qa, ka, va, cq, ckv, kr = jnp.split(p, SPLIT_POINTS, axis=-1)
    qa = qa.reshape(bt, n, H_A, DH_A)
    ka = ka.reshape(bt, n, KV_A, DH_A)
    va = va.reshape(bt, n, KV_A, DH_A)
    qb = jnp.einsum('bsr,re->bse', rmsnorm(cq, q_norm), w_q_up).reshape(bt, n, H_B, NOPE_B + ROPE_B)
    kvb = jnp.einsum('bsr,re->bse', rmsnorm(ckv, kv_norm), w_kv_up).reshape(bt, n, H_B, NOPE_B + V_B)
    return (qa, ka, va, qb[..., :NOPE_B], qb[..., NOPE_B:], kr,
            kvb[..., :NOPE_B], kvb[..., NOPE_B:])

def token_mixers(h, hc, rows, cols, w_in, sink, q_norm, kv_norm, w_q_up, w_kv_up, w_out, with_ctx_out):
    sink_g = sink.reshape(KV_A, G_A)
    qa, ka, va, qbn, qbr, kr, kbn, vb = project_groups(h, w_in, q_norm, kv_norm, w_q_up, w_kv_up)
    qa_c, ka_c, va_c, qbn_c, qbr_c, kr_c, kbn_c, vb_c = project_groups(hc, w_in, q_norm, kv_norm, w_q_up, w_kv_up)
    qa = axial_rope(qa, rows, cols)
    ka = axial_rope(ka, rows, cols)
    qbr = axial_rope(qbr, rows, cols)
    kr = axial_rope(kr[:, :, None, :], rows, cols)[:, :, 0, :]
    o_a = window_attention_latent(qa, ka, va, ka_c, va_c, sink_g)
    o_b = mla_latent(qbn, qbr,
                     jnp.concatenate([kbn_c, kbn], axis=1),
                     jnp.concatenate([kr_c, kr], axis=1),
                     jnp.concatenate([vb_c, vb], axis=1))
    out = jnp.einsum('bse,ed->bsd', jnp.concatenate([o_a, o_b], axis=-1), w_out)
    if not with_ctx_out:
        return out, None
    lc = hc.shape[1]
    o_a_c = gqa_sink_attend(qa_c.reshape(hc.shape[0], lc, KV_A, G_A, DH_A), ka_c, va_c, None, sink_g)
    o_b_c = mla_attend(qbn_c, qbr_c, kbn_c, kr_c, vb_c)
    out_c = jnp.einsum('bse,ed->bsd', jnp.concatenate([o_a_c, o_b_c], axis=-1), w_out)
    return out, out_c

def ec_moe(h, w_router, w_gate, w_up, w_down):
    n = h.shape[1]
    cap = CAP_FACTOR * n // N_EXPERTS
    aff = jax.nn.softmax(jnp.einsum('bnd,de->bne', h, w_router, preferred_element_type=jnp.float32), axis=-1)
    vals, idx = lax.top_k(jnp.swapaxes(aff, 1, 2), cap)

    def per_sample(hs, idx_s, val_s):
        xs = hs[idx_s]
        a = jnp.einsum('ecd,edf->ecf', xs, w_gate)
        u = jnp.einsum('ecd,edf->ecf', xs, w_up)
        y = jnp.einsum('ecf,efd->ecd', jax.nn.silu(a) * u, w_down) * val_s[..., None].astype(hs.dtype)
        return jnp.zeros_like(hs).at[idx_s.reshape(-1)].add(y.reshape(-1, hs.shape[-1]).astype(hs.dtype))

    return jax.vmap(per_sample)(h, idx, vals)

def first_inputs(seed: int = 0) -> dict:
    key = jax.random.key(seed)
    ks = jax.random.split(key, 20)
    f32 = jnp.float32
    L = DEPTH

    def nrm(k, shape, scale):
        return jax.random.normal(k, shape, f32) * scale

    return {
        "x": nrm(ks[0], (BATCH, SEQ, D_MODEL), 1.0),
        "c": nrm(ks[1], (BATCH, D_MODEL), 1.0),
        "ctx": nrm(ks[2], (BATCH, CTX_LEN, D_MODEL), 1.0),
        "c_ctx": nrm(ks[3], (D_MODEL,), 1.0),
        "w_mod": nrm(ks[4], (L, D_MODEL, 6 * D_MODEL), 0.5 * D_MODEL ** -0.5),
        "b_mod": nrm(ks[5], (L, 6 * D_MODEL), 0.01),
        "norm_attn": 1.0 + nrm(ks[6], (L, D_MODEL), 0.02),
        "norm_ffn": 1.0 + nrm(ks[7], (L, D_MODEL), 0.02),
        "w_in": nrm(ks[8], (L, D_MODEL, IN_DIM), D_MODEL ** -0.5),
        "sink": nrm(ks[9], (L, H_A), 0.5),
        "q_norm": 1.0 + nrm(ks[10], (L, Q_RANK), 0.02),
        "kv_norm": 1.0 + nrm(ks[11], (L, KV_RANK), 0.02),
        "w_q_up": nrm(ks[12], (L, Q_RANK, H_B * (NOPE_B + ROPE_B)), Q_RANK ** -0.5),
        "w_kv_up": nrm(ks[13], (L, KV_RANK, H_B * (NOPE_B + V_B)), KV_RANK ** -0.5),
        "w_out": nrm(ks[14], (L, MIX_DIM, D_MODEL), MIX_DIM ** -0.5),
        "w_router": nrm(ks[15], (L, D_MODEL, N_EXPERTS), D_MODEL ** -0.5),
        "w_gate": nrm(ks[16], (L, N_EXPERTS, D_MODEL, D_FF), D_MODEL ** -0.5),
        "w_up": nrm(ks[17], (L, N_EXPERTS, D_MODEL, D_FF), D_MODEL ** -0.5),
        "w_down": nrm(ks[18], (L, N_EXPERTS, D_FF, D_MODEL), D_FF ** -0.5),
        "norm_final": 1.0 + nrm(ks[19], (D_MODEL,), 0.02),
    }

def first_block(x, c, ctx, c_ctx, w_mod, b_mod, norm_attn, norm_ffn, w_in, sink, q_norm, kv_norm,
              w_q_up, w_kv_up, w_out, w_router, w_gate, w_up, w_down, norm_final):
    n_lat = x.shape[1]
    ROWS = n_lat // GRID_W
    rows = jnp.repeat(jnp.arange(ROWS, dtype=jnp.int32), GRID_W)
    cols = jnp.tile(jnp.arange(GRID_W, dtype=jnp.int32), ROWS)
    xc = ctx
    for l in range(DEPTH):
        last = l == DEPTH - 1
        mod = jnp.einsum('bd,de->be', jax.nn.silu(c), w_mod[l]) + b_mod[l]
        mod_c = jnp.einsum('d,de->e', jax.nn.silu(c_ctx), w_mod[l]) + b_mod[l]
        sh_a, sc_a, g_a, sh_f, sc_f, g_f = [m[:, None, :] for m in jnp.split(mod, 6, axis=-1)]
        csh_a, csc_a, cg_a, csh_f, csc_f, cg_f = jnp.split(mod_c, 6, axis=-1)

        h = modulate(rmsnorm(x, norm_attn[l]), sh_a, sc_a)
        hc = modulate(rmsnorm(xc, norm_attn[l]), csh_a, csc_a)
        mix, mix_c = token_mixers(h, hc, rows, cols, w_in[l], sink[l], q_norm[l], kv_norm[l],
                                  w_q_up[l], w_kv_up[l], w_out[l], not last)
        x = x + g_a * mix
        h2 = modulate(rmsnorm(x, norm_ffn[l]), sh_f, sc_f)
        x = x + g_f * ec_moe(h2, w_router[l], w_gate[l], w_up[l], w_down[l])

        if not last:
            xc = xc + cg_a * mix_c
            h2c = modulate(rmsnorm(xc, norm_ffn[l]), csh_f, csc_f)
            xc = xc + cg_f * ec_moe(h2c, w_router[l], w_gate[l], w_up[l], w_down[l])
    return rmsnorm(x, norm_final)


CHUNK = 64
GDN_HEADS = 4
GDN_DK = 128
GDN_DV = 128
GDN_CONV = 4
ATT_HEADS = 8
ATT_DH = 64
ATT_BAND = 9
REL_CLIP = 128
D_FF_2 = 2816
FFN_CONV = 3

KEY_A = GDN_HEADS * GDN_DK
VAL_A = GDN_HEADS * GDN_DV
WIDTH_B = ATT_HEADS * ATT_DH
IN_SIZES = (KEY_A, KEY_A, VAL_A, VAL_A, GDN_HEADS, GDN_HEADS,
            WIDTH_B, WIDTH_B, WIDTH_B, D_MODEL, D_MODEL)
IN_SPLITS = tuple(sum(IN_SIZES[:i + 1]) for i in range(len(IN_SIZES) - 1))
D_IN = sum(IN_SIZES)
CONV_A = 2 * KEY_A + VAL_A


def rmsnorm_2(x, w):
    xf = x.astype(jnp.float32)
    y = xf * lax.rsqrt(jnp.mean(xf * xf, axis=-1, keepdims=True) + EPS)
    return (y * w.astype(jnp.float32)).astype(x.dtype)

def l2norm(x):
    xf = x.astype(jnp.float32)
    return xf * lax.rsqrt(jnp.sum(xf * xf, axis=-1, keepdims=True) + EPS)

def causal_dwconv(x, w):
    width = w.shape[0]
    return lax.conv_general_dilated(
        x, w[:, None, :].astype(x.dtype), window_strides=(1,), padding=[(width - 1, 0)],
        dimension_numbers=('NWC', 'WIO', 'NWC'), feature_group_count=x.shape[-1])

def gated_delta_rule(q, k, v, g, beta):
    b_, t_, h_, dk = q.shape
    dv = v.shape[-1]
    n = t_ // CHUNK

    def to_chunks(a):
        return a.astype(jnp.float32).reshape(b_, n, CHUNK, h_, -1).transpose(1, 0, 3, 2, 4)

    q = to_chunks(q) * (dk ** -0.5)
    k = to_chunks(k)
    v = to_chunks(v)
    g = g.astype(jnp.float32).reshape(b_, n, CHUNK, h_).transpose(1, 0, 3, 2)
    beta = beta.astype(jnp.float32).reshape(b_, n, CHUNK, h_).transpose(1, 0, 3, 2)

    G = jnp.cumsum(g, axis=-1)
    idx = jnp.arange(CHUNK)
    strict = idx[:, None] > idx[None, :]
    incl = idx[:, None] >= idx[None, :]
    diff = G[..., :, None] - G[..., None, :]
    dec_strict = jnp.exp(jnp.where(strict, diff, -jnp.inf))
    dec_incl = jnp.exp(jnp.where(incl, diff, -jnp.inf))
    gam = jnp.exp(G)

    a_mat = beta[..., :, None] * jnp.einsum('nbhid,nbhjd->nbhij', k, k) * dec_strict
    eye = jnp.eye(CHUNK, dtype=jnp.float32)
    rhs = jnp.concatenate([(beta * gam)[..., None] * k, beta[..., None] * v], axis=-1)
    sol = lax.linalg.triangular_solve(a_mat + eye, rhs, left_side=True, lower=True)
    w_c = sol[..., :dk]
    uv_c = sol[..., dk:]
    p_c = jnp.einsum('nbhid,nbhjd->nbhij', q, k) * dec_incl
    qg_c = q * gam[..., None]
    kd_c = k * jnp.exp(G[..., -1:] - G)[..., None]
    gl_c = gam[..., -1]

    def step(s, xs):
        w_i, uv_i, p_i, qg_i, kd_i, gl_i = xs
        u = uv_i - jnp.einsum('bhid,bhde->bhie', w_i, s)
        o = jnp.einsum('bhid,bhde->bhie', qg_i, s) + jnp.einsum('bhij,bhje->bhie', p_i, u)
        s = gl_i[..., None, None] * s + jnp.einsum('bhid,bhie->bhde', kd_i, u)
        return s, o

    s0 = jnp.zeros((b_, h_, dk, dv), jnp.float32)
    _, o = lax.scan(step, s0, (w_c, uv_c, p_c, qg_c, kd_c, gl_c))
    return o.transpose(1, 0, 3, 2, 4).reshape(b_, t_, h_, dv)

def chunk_band_attention(q, k, v, rel_table):
    b_, t_, h_, dh = q.shape
    n = t_ // CHUNK
    band = ATT_BAND * CHUNK
    lead = (ATT_BAND - 1) * CHUNK
    kp = jnp.pad(k, ((0, 0), (lead, 0), (0, 0), (0, 0)))
    vp = jnp.pad(v, ((0, 0), (lead, 0), (0, 0), (0, 0)))
    r = jnp.arange(CHUNK)
    j = jnp.arange(band)
    dist = lead + r[:, None] - j[None, :]
    bias = rel_table.astype(jnp.float32)[:, jnp.clip(dist, -REL_CLIP, REL_CLIP) + REL_CLIP]
    scale = dh ** -0.5

    def one_chunk(c):
        start = c * CHUNK
        qc = lax.dynamic_slice_in_dim(q, start, CHUNK, axis=1)
        kc = lax.dynamic_slice_in_dim(kp, start, band, axis=1)
        vc = lax.dynamic_slice_in_dim(vp, start, band, axis=1)
        s = jnp.einsum('bqhd,bkhd->bhqk', qc, kc).astype(jnp.float32) * scale + bias
        valid = j >= lead - start
        s = jnp.where(valid[None, None, None, :], s, -jnp.inf)
        p = jax.nn.softmax(s, axis=-1).astype(v.dtype)
        return jnp.einsum('bhqk,bkhd->bqhd', p, vc)

    out = lax.map(one_chunk, jnp.arange(n))
    return out.transpose(1, 0, 2, 3, 4).reshape(b_, t_, h_ * dh)

def second_inputs(seed: int = 0) -> dict:
    key = jax.random.key(seed)
    ks = jax.random.split(key, 20)
    f32 = jnp.float32
    nrm = lambda k, shape, s: jax.random.normal(k, shape, f32) * s
    gain = lambda k, shape: 1.0 + 0.02 * jax.random.normal(k, shape, f32)
    dt = jnp.exp(jax.random.uniform(ks[4], (DEPTH, GDN_HEADS), f32, np.log(1e-3), np.log(1e-1)))
    return {
        "x": nrm(ks[0], (BATCH, SEQ, D_MODEL), 1.0),
        "norm_mix_w": gain(ks[1], (DEPTH, D_MODEL)),
        "w_in": nrm(ks[2], (DEPTH, D_MODEL, D_IN), D_MODEL ** -0.5),
        "conv_qkv_w": nrm(ks[3], (DEPTH, GDN_CONV, CONV_A), GDN_CONV ** -0.5),
        "a_log": jnp.log(jax.random.uniform(ks[5], (DEPTH, GDN_HEADS), f32, 1.0, 16.0)),
        "dt_bias": dt + jnp.log(-jnp.expm1(-dt)),
        "gdn_norm_w": gain(ks[6], (DEPTH, GDN_DV)),
        "w_branch_a": nrm(ks[7], (DEPTH, VAL_A, D_MODEL), VAL_A ** -0.5),
        "w_branch_b": nrm(ks[8], (DEPTH, WIDTH_B, D_MODEL), WIDTH_B ** -0.5),
        "rel_bias": nrm(ks[9], (DEPTH, ATT_HEADS, 2 * REL_CLIP + 1), 0.5),
        "w_out": nrm(ks[10], (DEPTH, D_MODEL, D_MODEL), D_MODEL ** -0.5),
        "norm_ffn_w": gain(ks[11], (DEPTH, D_MODEL)),
        "w_up": nrm(ks[12], (DEPTH, D_MODEL, 2 * D_FF_2), D_MODEL ** -0.5),
        "conv_ffn_w": nrm(ks[13], (DEPTH, FFN_CONV, 2 * D_FF_2), FFN_CONV ** -0.5),
        "conv_ffn_b": nrm(ks[14], (DEPTH, 2 * D_FF_2), 0.02),
        "w_down": nrm(ks[15], (DEPTH, D_FF_2, D_MODEL), D_FF_2 ** -0.5),
        "norm_final_w": gain(ks[16], (D_MODEL,)),
    }

def second_block(x, norm_mix_w, w_in, conv_qkv_w, a_log, dt_bias, gdn_norm_w, w_branch_a, w_branch_b,
              rel_bias, w_out, norm_ffn_w, w_up, conv_ffn_w, conv_ffn_b, w_down, norm_final_w):
    b_, t_, _ = x.shape
    for l in range(DEPTH):
        h = rmsnorm_2(x, norm_mix_w[l])
        proj = h @ w_in[l]
        qa, ka, va, za, ba, aa, qb, kb, vb, ga, gb = jnp.split(proj, IN_SPLITS, axis=-1)

        qkv = jax.nn.silu(causal_dwconv(jnp.concatenate([qa, ka, va], axis=-1), conv_qkv_w[l]))
        qa, ka, va = jnp.split(qkv, (KEY_A, 2 * KEY_A), axis=-1)
        qa = l2norm(qa.reshape(b_, t_, GDN_HEADS, GDN_DK))
        ka = l2norm(ka.reshape(b_, t_, GDN_HEADS, GDN_DK))
        va = va.reshape(b_, t_, GDN_HEADS, GDN_DV)
        beta = jax.nn.sigmoid(ba.astype(jnp.float32))
        g = -jnp.exp(a_log[l].astype(jnp.float32)) * jax.nn.softplus(
            aa.astype(jnp.float32) + dt_bias[l].astype(jnp.float32))
        oa = gated_delta_rule(qa, ka, va, g, beta)
        za = za.reshape(b_, t_, GDN_HEADS, GDN_DV).astype(jnp.float32)
        oa = (rmsnorm_2(oa, gdn_norm_w[l]) * jax.nn.silu(za)).astype(x.dtype).reshape(b_, t_, VAL_A)

        ob = chunk_band_attention(qb.reshape(b_, t_, ATT_HEADS, ATT_DH),
                                  kb.reshape(b_, t_, ATT_HEADS, ATT_DH),
                                  vb.reshape(b_, t_, ATT_HEADS, ATT_DH), rel_bias[l])

        mix = jax.nn.sigmoid(ga) * (oa @ w_branch_a[l]) + jax.nn.sigmoid(gb) * (ob @ w_branch_b[l])
        x = x + mix @ w_out[l]

        h = rmsnorm_2(x, norm_ffn_w[l])
        u = causal_dwconv(h @ w_up[l], conv_ffn_w[l]) + conv_ffn_b[l]
        gate, up = jnp.split(u, 2, axis=-1)
        x = x + (jax.nn.silu(gate) * up) @ w_down[l]
    return rmsnorm_2(x, norm_final_w)


def setup_inputs(seed=0):
    out = dict(first_inputs(seed))
    for name, value in second_inputs(seed + 1).items():
        if name != "x":
            out[name + "_2"] = value
    return out


def reference(
    x, c, ctx, c_ctx, w_mod, b_mod, norm_attn, norm_ffn, w_in, sink, q_norm, kv_norm, w_q_up,
    w_kv_up, w_out, w_router, w_gate, w_up, w_down, norm_final, norm_mix_w_2, w_in_2,
    conv_qkv_w_2, a_log_2, dt_bias_2, gdn_norm_w_2, w_branch_a_2, w_branch_b_2, rel_bias_2,
    w_out_2, norm_ffn_w_2, w_up_2, conv_ffn_w_2, conv_ffn_b_2, w_down_2, norm_final_w_2,
):
    x = first_block(
        x, c, ctx, c_ctx, w_mod, b_mod, norm_attn, norm_ffn, w_in, sink, q_norm, kv_norm,
        w_q_up, w_kv_up, w_out, w_router, w_gate, w_up, w_down, norm_final,
    )
    return second_block(
        x, norm_mix_w_2, w_in_2, conv_qkv_w_2, a_log_2, dt_bias_2, gdn_norm_w_2, w_branch_a_2,
        w_branch_b_2, rel_bias_2, w_out_2, norm_ffn_w_2, w_up_2, conv_ffn_w_2, conv_ffn_b_2,
        w_down_2, norm_final_w_2,
    )


_drawn_inputs = setup_inputs


def setup_inputs(seed=0):
    import zlib

    import numpy as np

    out = dict(_drawn_inputs(seed))
    spreads = {}
    factors = {'ctx': 2.696,
     'b_mod': 6.66,
     'norm_attn': 8.0,
     'norm_ffn': 6.896,
     'sink': 8.0,
     'q_norm': 8.0,
     'kv_norm': 8.0,
     'w_q_up': 2.856,
     'norm_mix_w_2': 4.714,
     'gdn_norm_w_2': 7.558,
     'norm_ffn_w_2': 13.36,
     'conv_ffn_b_2': 14.256,
     'norm_final_w_2': 7.48,
     'rel_bias_2': 3.419}
    for name, (base, spread) in spreads.items():
        noise = np.random.default_rng([zlib.crc32(name.encode()), seed]).standard_normal(out[name].shape)
        drawn = base * np.exp(spread * noise) if base else spread * noise
        out[name] = __import__('jax').numpy.asarray(drawn.astype(out[name].dtype))
    for name, factor in factors.items():
        out[name] = (out[name] * factor).astype(out[name].dtype)
    return out
```

```python
import numpy as np
import concourse.bass as bass
from concourse import mybir

F32 = mybir.dt.float32
BF16 = mybir.dt.bfloat16
U32 = mybir.dt.uint32
I32 = mybir.dt.int32
ALU = mybir.AluOpType
ACT = mybir.ActivationFunctionType
AX = mybir.AxisListType

P = 128
D = 1024
KD = D // P
SEQ, CTX = 1024, 256
NT, NC = SEQ // P, CTX // P
NK = NT + NC
BANK = 512
EPS = 1e-6
NEG = -1e30

HA, GA_, DA = 8, 4, 64
HB, NOPE, ROPE, VB_ = 8, 64, 32, 64
QKB = NOPE + ROPE
QR, KVR = 384, 256
KQ, KKV = QR // P, KVR // P
W_Q, W_K, W_V, W_CKV, W_KR, W_CQ = 0, 512, 640, 768, 1024, 1056
W_IN = 1440
NE, CAP, FF = 16, 128, 512
KF = FF // P
GH, GDK = 4, 128
CHUNK = 64
HS, DS = 8, 64
LEAD = 512
FF2 = 2816
NF2 = FF2 // P


class Chain:

    def __init__(self, eng, sem):
        self.eng, self.sem, self.n = eng, sem, 0

    def put(self, ins):
        ins.then_inc(self.sem, 1)
        self.n += 1

    def wait(self):
        self.eng.wait_ge(self.sem, self.n)

    def __call__(self, ins):
        self.put(ins)
        self.wait()


class Core:

    def __init__(self, nc):
        self.nc = nc
        self.ps = nc.alloc_psum_tensor("banks", [P, 8 * BANK], F32)
        self.base = -(-nc.sbuf_base // 64) * 64
        self.words = (nc.sbuf_usable_end - self.base) // 32 * 8

        self.mine = []

    def sem(self, name):
        self.mine.append(self.nc.alloc_semaphore(name))
        return self.mine[-1]

    def kept_sem(self, name):
        return self.nc.alloc_semaphore(name)

    def recycle(self):
        self.nc.clear_and_free_semaphores(self.mine)
        self.nc.all_engine_barrier()
        self.mine = []

    def area(self, name, at, *shape, dtype=F32, parts=P):
        n = int(np.prod(shape)) * (2 if dtype == BF16 else 4) // 4
        assert at + n <= self.words, (name, at, n, self.words)
        return self.nc.alloc_sbuf_tensor_at(name, [parts, *shape], dtype, offset=self.base + 4 * at)

    def bank(self, b, n=BANK):
        return self.ps[:, BANK * b:BANK * b + n]


def transpose_groups(c, name, groups, ident):
    nc = c.nc
    tp, by_act, by_dve = (c.sem(f"{name}_{x}") for x in ("transposed", "out_act", "out_dve"))

    with nc.Block(no_gpsimd_drain=True) as block:
        @block.tensor
        def _(pe):
            for i, (pieces, target, _, _) in enumerate(groups):
                if i >= 8:
                    pe.wait_ge((by_act, by_dve)[i % 2], (i - 8) // 2 + 1)
                for j, piece in enumerate(pieces):
                    m = target.shape[0]
                    last = nc.tensor.transpose(c.ps[0:m, BANK * (i % 8) + P * j:BANK * (i % 8) + P * j + P],
                                               piece, ident[:, :])
                last.then_inc(tp, 1)

        @block.scalar
        def _(act):
            for i in range(0, len(groups), 2):
                pieces, target, scale, shift = groups[i]
                act.wait_ge(tp, i + 1)
                src = c.ps[0:target.shape[0], BANK * (i % 8):BANK * (i % 8) + P * len(pieces)]
                nc.scalar.activation(target, src, ACT.Identity, scale=1.0 if scale is None else scale,
                                     bias=0.0 if shift is None else shift).then_inc(by_act, 1)

        @block.vector
        def _(dve):
            for i in range(1, len(groups), 2):
                pieces, target, scale, shift = groups[i]
                dve.wait_ge(tp, i + 1)
                src = c.ps[0:target.shape[0], BANK * (i % 8):BANK * (i % 8) + P * len(pieces)]
                if shift is not None:
                    ins = nc.vector.tensor_scalar(target, src, scale, shift, ALU.mult, ALU.add)
                elif scale is not None:
                    ins = nc.vector.tensor_scalar(target, src, scale, None, ALU.mult)
                else:
                    ins = nc.vector.tensor_copy(target, src)
                ins.then_inc(by_dve, 1)


def norm_tokens(c, name, x, xn, n, eps, junk, stat, before=None, arrived=None, turn=1):
    nc = c.nc
    sq, ms, sd, link = (c.sem(f"{name}_{s}") for s in ("squares", "mean", "root", "link"))

    with nc.Block(no_gpsimd_drain=True) as block:
        if before is not None:
            block.sync(before)

        @block.scalar
        def _(act):
            for t in range(n):
                if arrived is not None:
                    act.wait_ge(arrived[t], 16 * turn)
                if t:
                    act.wait_ge(sq, t)
                nc.scalar.activation(junk[:, :], x[:, t, :], ACT.Square, scale=D ** -0.5,
                                     accum_out=stat[:, 0, t:t + 1]).then_inc(sq, 1)
            act.wait_ge(sq, n)
            nc.scalar.activation(stat[:, 1, 0:n], stat[:, 0, 0:n], ACT.Sqrt, bias=eps[:, 0:1]).then_inc(sd, 1)

        @block.vector
        def _(dve):
            step = Chain(dve, link)
            dve.wait_ge(sd, 1)
            step(nc.vector.reciprocal(stat[:, 2, 0:n], stat[:, 1, 0:n]))
            for t in range(n):
                nc.vector.tensor_scalar(xn[:, t, :], x[:, t, :], stat[:, 2, t:t + 1], None, ALU.mult)


def mod_vectors(c, k, d):
    nc = c.nc
    cin, constants, wm_in = c.sem("cond_in"), k.const_in, [c.sem(f"wmod_in{i}") for i in range(4)]
    silu, spread, col, row, read, link = (c.sem(f"mod_{s}") for s in
                                          ("silu", "spread", "columns", "rows", "read", "link"))
    k.tile_in = [c.kept_sem(f"tile_in{t}") for t in range(NK)]
    ring = c.area("wmod_ring", k.F, 4, KD, BANK)
    NCOL = 8

    with nc.Block(no_gpsimd_drain=True) as block:
        @block.sync
        def _(sp):
            sp.dma_start(k.cond[:, :, :], d["cond"]).then_inc(cin, 16)
            for s in range(12):
                if s >= 4:
                    if s - 4 < NCOL:
                        sp.wait_ge(col, s - 3)
                    else:
                        sp.wait_ge(row, s - 3 - NCOL)
                sp.dma_start(ring[:, s % 4, :, :], d["w_mod"][s]).then_inc(wm_in[s % 4], 16)
                if s == 0:
                    for dst, src in k.constants:
                        sp.dma_start(dst, src).then_inc(constants, 16)

        @block.scalar
        def _(act):
            act.wait_ge(cin, 16)
            nc.scalar.activation(k.silu_c[:, :, :], k.cond[:, :, :], ACT.Silu).then_inc(silu, 1)

        @block.vector
        def _(dve):
            step = Chain(dve, link)
            nc.vector.memset(k.eps[:, :], EPS)
            dve.wait_ge(silu, 1)
            nc.vector.tensor_copy(k.silu_rows[:, :, :], k.silu_c[:, :, 0:1].to_broadcast([P, KD, P])).then_inc(spread, 1)
            dve.wait_ge(constants, 16 * len(k.constants))
            dve.wait_ge(col, NCOL)
            step(nc.vector.tensor_tensor(k.mod[:, :, :], c.ps[:, 0:64].rearrange("p (m s) -> p m s", s=2),
                                         k.b_mod[:, :].unsqueeze(2).to_broadcast([P, 32, 2]), ALU.add))
            for w, m, s, to in ((k.norm_attn, 8, 0, k.scale_a), (k.norm_attn, 8, 1, k.scale_ac), (k.norm_ffn, 24, 0, k.scale_f)):
                nc.vector.scalar_tensor_tensor(to[:, :], k.mod[:, m:m + 8, s], 1.0, w[:, :], ALU.add, ALU.mult)
            for g in range(4):
                dve.wait_ge(row, g + 1)
                to = (k.gate_a, k.gate_f)[g // 2][:, BANK * (g % 2):BANK * (g % 2 + 1)]
                nc.vector.tensor_tensor(to, c.bank(1 + g), to, ALU.add)

        @block.tensor
        def _(pe):
            pe.wait_ge(silu, 1)
            for s in range(12):
                pe.wait_ge(wm_in[s % 4], 16 * (s // 4 + 1))
                if s < NCOL:
                    for b in range(4):
                        m = 4 * s + b
                        for q in range(KD):
                            last = nc.tensor.matmul(c.ps[:, 2 * m:2 * m + 2], ring[:, s % 4, q, P * b:P * b + P],
                                                    k.silu_c[:, q, :], start=q == 0, stop=q == KD - 1)
                    last.then_inc(col, 1)
                else:
                    if s == NCOL:
                        pe.wait_ge(spread, 1)
                    for q in range(KD):
                        last = nc.tensor.matmul(c.bank(1 + s - NCOL), k.silu_rows[:, q, :], ring[:, s % 4, q, :],
                                                start=q == 0, stop=q == KD - 1)
                    last.then_inc(row, 1)


def project_in(c, k, d):
    nc = c.nc
    mm, vec, copied, sq, scaled, sd, rs, link, turn = (c.sem(f"in_{s}") for s in
                                                       ("product", "rotated", "copied", "squares", "scaled", "root", "recip", "banks", "link"))
    SET = 4 * BANK
    with nc.Block(no_gpsimd_drain=True) as block:
        @block.tensor
        def _(pe):
            for t in range(NK):
                if t == 0:
                    pe.wait_ge(k.w_in_in, 16)
                if t >= 2:
                    pe.wait_ge(vec, 3 * (t - 1))
                    pe.wait_ge(copied, t - 1)
                base = (t % 2) * SET
                h = k.hT[:, :, P * t:P * t + P] if t < NT else k.hcT[:, :, P * (t - NT):P * (t - NT) + P]
                cuts = [(0, 512), (512, 1024), (1024, W_IN)] if t < NT else [(512, 1024), (1024, W_CQ)]
                for a, b in cuts:
                    for q in range(KD):
                        last = nc.tensor.matmul(c.ps[:, base + a:base + b], h[:, q, :], k.w_in[:, q, a:b],
                                                start=q == 0, stop=q == KD - 1)
                last.then_inc(mm, 1)

        @block.vector
        def _(dve):
            step = Chain(dve, turn)

            def rotate(out, src, tmp, table, heads, nf):
                s4 = src.rearrange("p (h a s f) -> p h a s f", h=heads, a=2, s=2)
                t4 = tmp.rearrange("p (h a s f) -> p h a s f", h=heads, a=2, s=2)
                cos = table[:, 0, :].unsqueeze(1).to_broadcast([P, heads, 4 * nf])
                step.put(nc.vector.tensor_tensor(out.rearrange("p (h e) -> p h e", h=heads),
                                                 src.rearrange("p (h e) -> p h e", h=heads), cos, ALU.mult))
                sin = table[:, 1, :].rearrange("p (a s f) -> p a s f", a=2, s=2)
                for s in range(2):
                    step.put(nc.vector.tensor_tensor(t4[:, :, :, s, :], s4[:, :, :, 1 - s, :],
                                                     sin[:, :, s, :].unsqueeze(1).to_broadcast([P, heads, 2, nf]), ALU.mult))
                step.wait()
                return nc.vector.tensor_tensor(out, out, tmp, ALU.add)

            for t in range(NK):
                raw = k.raw[:, t % 2, :]
                kr = k.kr_key[:, (t + NC) % NK, :]
                if t:
                    dve.wait_ge(vec, 3 * t)
                dve.wait_ge(mm, t + 1)
                if t < NT:
                    rotate(k.qk_tok[:, t, 0:512], c.ps[:, (t % 2) * SET:(t % 2) * SET + 512], k.tmp[:, 0:512], k.rope_a[:, t], 8, 16).then_inc(vec, 1)
                    dve.wait_ge(copied, t + 1)
                    rotate(k.qk_tok[:, t, 512:640], raw[:, 0:128], k.tmp[:, 512:640], k.rope_a[:, t], 2, 16).then_inc(vec, 1)
                    rotate(kr, raw[:, 512:544], k.tmp[:, 640:672], k.rope_b[:, t], 1, 8).then_inc(vec, 1)
                else:
                    dve.wait_ge(copied, t + 1)
                    nc.vector.tensor_copy(k.qk_tok[:, t, 512:640], raw[:, 0:128]).then_inc(vec, 1)
                    nc.vector.tensor_copy(kr, raw[:, 512:544]).then_inc(vec, 2)
                dve.wait_ge(sd, t + 1)
                nc.vector.reciprocal(k.lstat[:, 2, t, 0:2 if t < NT else 1], k.lstat[:, 1, t, 0:2 if t < NT else 1]).then_inc(rs, 1)

        @block.scalar
        def _(act):
            n_sq = 0
            for t in range(NK):
                base = (t % 2) * SET
                raw = k.raw[:, t % 2, :]
                act.wait_ge(mm, t + 1)
                if t >= 2:
                    act.wait_ge(vec, 3 * (t - 1))
                    act.wait_ge(scaled, t - 1)
                nc.scalar.activation(raw[:, 0:512], c.ps[:, base + 512:base + 1024], ACT.Identity).then_inc(link, 1)
                width = 416 if t < NT else 32
                nc.scalar.activation(raw[:, 512:512 + width], c.ps[:, base + 1024:base + 1024 + width], ACT.Identity).then_inc(copied, 1)
                act.wait_ge(copied, t + 1)
                nc.scalar.activation(k.v_a[:, (t + NC) % NK, :], raw[:, 128:256], ACT.Identity)
                parts = [(256, KVR, 0), (544, QR, 1)][:2 if t < NT else 1]
                for a, n, s in parts:
                    if n_sq:
                        act.wait_ge(sq, n_sq)
                    nc.scalar.activation(k.junk[:, 0:n], raw[:, a:a + n], ACT.Square,
                                         scale=n ** -0.5, accum_out=k.lstat[:, 0, t, s:s + 1]).then_inc(sq, 1)
                    n_sq += 1
                act.wait_ge(sq, n_sq)
                nc.scalar.activation(k.lstat[:, 1, t, 0:len(parts)], k.lstat[:, 0, t, 0:len(parts)], ACT.Sqrt,
                                     bias=k.eps[:, 0:1]).then_inc(sd, 1)
                act.wait_ge(rs, t + 1)
                for a, n, s in parts:
                    last = nc.scalar.activation(k.lat_tok[:, t, 256 * s:256 * s + n], raw[:, a:a + n],
                                                ACT.Identity, scale=k.lstat[:, 2, t, s:s + 1])
                last.then_inc(scaled, 1)


def project_up(c, k, d, which):
    nc = c.nc
    mm, act_done, vec, kr, link = (c.sem(f"up{which}_{s}") for s in ("product", "copied", "rotated", "shared", "link"))
    n = NT if which == "q" else NK
    with nc.Block(no_gpsimd_drain=True) as block:
        @block.tensor
        def _(pe):
            pe.wait_ge(k.up_in[which], 16)
            for t in range(n):
                if t >= 4:
                    pe.wait_ge(vec, t - 3)
                    pe.wait_ge(act_done, t - 3)
                base = (t % 4) * 2 * BANK
                lat, w, nk, width = (k.cqT, k.w_q_up, KQ, 768) if which == "q" else (k.ckvT, k.w_kv_up, KKV, 1024)
                for a in range(0, width, 512):
                    b = min(a + 512, width)
                    for q in range(nk):
                        last = nc.tensor.matmul(c.ps[:, base + a:base + b], lat[:, q, P * t:P * t + P], w[:, q, a:b],
                                                start=q == 0, stop=q == nk - 1)
                last.then_inc(mm, 1)

        @block.scalar
        def _(act):
            for t in range(n):
                act.wait_ge(mm, t + 1)
                base = (t % 4) * 2 * BANK
                if which == "q":
                    nc.scalar.activation(k.b_tok[:, t, :, :], c.ps[:, base:base + 768].rearrange("p (h e) -> p h e", h=HB),
                                         ACT.Identity).then_inc(act_done, 1)
                else:
                    nc.scalar.activation(k.v_b[:, t, :], c.ps[:, base + 512:base + 1024], ACT.Identity).then_inc(act_done, 1)

        @block.vector
        def _(dve):
            step = Chain(dve, link)
            for t in range(n):
                dve.wait_ge(mm, t + 1)
                base = (t % 4) * 2 * BANK
                if which == "q":
                    if t:
                        dve.wait_ge(vec, t)
                    dve.wait_ge(act_done, t + 1)
                    src = k.b_tok[:, t, :, NOPE:QKB]
                    out = k.tmp[:, 256:512].rearrange("p (h e) -> p h e", h=HB)
                    s4 = src.rearrange("p h (a s f) -> p h a s f", a=2, s=2)
                    o4 = k.tmp[:, 0:256].rearrange("p (h a s f) -> p h a s f", h=HB, a=2, s=2)
                    table = k.rope_b[:, t]
                    step.put(nc.vector.tensor_tensor(out, src, table[:, 0, :].unsqueeze(1).to_broadcast([P, HB, ROPE]), ALU.mult))
                    sin = table[:, 1, :].rearrange("p (a s f) -> p a s f", a=2, s=2)
                    for s in range(2):
                        step.put(nc.vector.tensor_tensor(o4[:, :, :, s, :], s4[:, :, :, 1 - s, :],
                                                         sin[:, :, s, :].unsqueeze(1).to_broadcast([P, HB, 2, 8]), ALU.mult))
                    step.wait()
                    nc.vector.tensor_tensor(src, out, k.tmp[:, 0:256].rearrange("p (h e) -> p h e", h=HB), ALU.add).then_inc(vec, 1)
                else:
                    nc.vector.tensor_copy(k.b_tok[:, t, :, 0:NOPE],
                                          c.ps[:, base:base + 512].rearrange("p (h e) -> p h e", h=HB)).then_inc(vec, 1)

        if which == "kv":
            @block.gpsimd
            def _(pool):
                src = k.kr_key[:, :, :].unsqueeze(2).to_broadcast([P, NK, HB, ROPE])
                for t in range(n):
                    nc.gpsimd.tensor_copy(k.b_tok[:, t, :, NOPE:QKB], src[:, t]).then_inc(kr, 1)
                pool.wait_ge(kr, n)


class Unit:

    def __init__(self, q, keys, values, out, masks=(), sink=None, bias=None):
        self.q, self.keys, self.values, self.out = q, keys, values, out
        self.masks, self.sink, self.bias = masks, sink, bias
        self.n = P * len(values)


def attend(c, k, name, units, sets, banks, p, pre=None, before=None, bias_in=None, bias_free=None):
    nc = c.nc
    scored, negmax, exped, turned, out_act, out_dve, mixed, scaled, sunk, link = (
        c.sem(f"{name}_{s}") for s in ("scored", "negmax", "exped", "turned", "out_act", "out_dve", "mixed", "scaled", "sunk", "link"))
    n, ahead = len(units), sets - 1
    nt = max(u.n for u in units)
    prob, probT, st = p
    pieces, count = [], [0, 0]
    for u, unit in enumerate(units):
        tiles = unit.n // P
        for a in range(0, tiles, 4):
            e = 0 if a == 0 else 1
            count[e] += 1
            pieces.append((u, a, min(4, tiles - a), e, count[e]))
    of_unit = [[(g, x) for g, x in enumerate(pieces) if x[0] == u] for u in range(n)]
    TURN = 8 - 2

    def scores(u):
        return c.ps[:, (u % sets) * banks * BANK:(u % sets) * banks * BANK + units[u].n]

    uses = []
    use_of_product, use_of_piece = {}, {}
    for s in range(n + 1):
        if s:
            use_of_product[s - 1] = len(uses)
            uses.append((scaled, s))
        for g, x in of_unit[s] if s < n else ():
            use_of_piece[g] = len(uses)
            uses.append(((out_dve, out_act)[x[3]], x[4]))

    def turn_bank(r, m):
        return c.ps[:, BANK * (TURN + r % 2):BANK * (TURN + r % 2) + m]

    def product(u):
        return turn_bank(use_of_product[u], 64)

    with nc.Block(no_gpsimd_drain=True) as block:
        if before is not None:
            block.sync(before)

        @block.tensor
        def _(pe):
            for s in range(-ahead, n + 1):
                u = s + ahead
                if u < n:
                    if u >= sets:
                        pe.wait_ge(exped if pre is None else negmax, u - sets + 1)
                    out, unit = scores(u), units[u]
                    for a, key in unit.keys:
                        m = key.shape[-1]
                        masks = [x for x in unit.masks if a <= x[0] < a + m]
                        last = nc.tensor.matmul(out[:, a:a + m], unit.q, key, start=True, stop=not masks)
                        for i, (at, mask) in enumerate(masks):
                            last = nc.tensor.matmul(out[:, at:at + P], k.ident_bf[:, :], mask, start=False,
                                                    stop=i == len(masks) - 1)
                    last.then_inc(scored, 1)
                if 0 <= s - 1:
                    v = s - 1
                    for e in range(2):
                        mine = [x[4] for _, x in of_unit[v] if x[3] == e]
                        if mine:
                            pe.wait_ge((out_dve, out_act)[e], mine[-1])
                    if use_of_product[v] >= 2:
                        pe.wait_ge(*uses[use_of_product[v] - 2])
                    for j, val in enumerate(units[v].values):
                        last = nc.tensor.matmul(product(v), probT[:, v % 2, P * j:P * j + P], val, start=j == 0,
                                                stop=j == len(units[v].values) - 1)
                    last.then_inc(mixed, 1)
                if 0 <= s < n:
                    pe.wait_ge(exped, s + 1)
                    for g, (_, a, m, _, _) in of_unit[s]:
                        if use_of_piece[g] >= 2:
                            pe.wait_ge(*uses[use_of_piece[g] - 2])
                        for j in range(m):
                            last = nc.tensor.transpose(turn_bank(use_of_piece[g], P * m)[:, P * j:P * j + P],
                                                       prob[:, s % 2, P * (a + j):P * (a + j) + P], k.ident[:, :])
                        last.then_inc(turned, 1)

        def piece_out(eng, s, e, copy):
            for g, (_, a, m, by, _) in of_unit[s]:
                if by == e:
                    eng.wait_ge(turned, g + 1)
                    if s >= 2:
                        eng.wait_ge(mixed, s - 1)
                    copy(probT[:, s % 2, P * a:P * (a + m)],
                         turn_bank(use_of_piece[g], P * m)).then_inc((out_dve, out_act)[e], 1)

        @block.vector
        def _(dve):
            step = Chain(dve, link)
            for s in range(-ahead, n + 1):
                u = s + ahead
                if u < n:
                    unit, col = units[u], st[:, u % 8, :]
                    dve.wait_ge(scored, u + 1)
                    if u >= 8:
                        dve.wait_ge(scaled, u - 7)
                    if pre is None:
                        step(nc.vector.reduce_max(col[:, 0:1], scores(u), AX.X))
                    else:
                        if u >= 2:
                            dve.wait_ge(exped, u - 1)
                        if unit.bias[0] is not None:
                            dve.wait_ge(*unit.bias[0])
                        ins = nc.vector.tensor_tensor_reduce(out=pre[:, u % 2, 0:unit.n], in0=scores(u), in1=unit.bias[1],
                                                             scale=1.0, scalar=NEG, op0=ALU.add, op1=ALU.max,
                                                             accum_out=col[:, 0:1])
                        step(ins)
                    if unit.sink is None:
                        nc.vector.tensor_scalar(col[:, 1:2], col[:, 0:1], -1.0, None, ALU.mult).then_inc(negmax, 1)
                    else:
                        step(nc.vector.tensor_tensor(col[:, 0:1], col[:, 0:1], unit.sink, ALU.max))
                        nc.vector.tensor_scalar(col[:, 1:2], col[:, 0:1], -1.0, None, ALU.mult).then_inc(negmax, 1)
                if 0 <= s - 1:
                    v = s - 1
                    unit, col = units[v], st[:, v % 8, :]
                    dve.wait_ge(exped, v + 1)
                    if unit.sink is not None:
                        dve.wait_ge(sunk, v + 1)
                        step(nc.vector.tensor_tensor(col[:, 2:3], col[:, 2:3], col[:, 3:4], ALU.add))
                    step(nc.vector.reciprocal(col[:, 0:1], col[:, 2:3]))
                    dve.wait_ge(mixed, v + 1)
                    nc.vector.tensor_scalar(unit.out, product(v), col[:, 0:1], None, ALU.mult).then_inc(scaled, 1)
                if 0 <= s < n:
                    piece_out(dve, s, 0, nc.vector.tensor_copy)

        @block.scalar
        def _(act):
            for s in range(-ahead, n):
                if s >= 0:
                    piece_out(act, s, 1, lambda o, i: nc.scalar.activation(o, i, ACT.Identity))
                u = s + ahead
                if u < n:
                    unit, col = units[u], st[:, u % 8, :]
                    act.wait_ge(negmax, u + 1)
                    if unit.sink is not None:
                        nc.scalar.activation(col[:, 3:4], unit.sink, ACT.Exp, bias=col[:, 1:2]).then_inc(sunk, 1)
                    if u >= 2:
                        act.wait_ge(turned, of_unit[u - 2][-1][0] + 1)
                    nc.scalar.activation(prob[:, u % 2, 0:unit.n], scores(u) if pre is None else pre[:, u % 2, 0:unit.n],
                                         ACT.Exp, bias=col[:, 1:2], accum_out=col[:, 2:3]).then_inc(exped, 1)


def mix_out(c, k, name, aT, w, w_in_sem, gate, turn, x, out, before=None):
    nc = c.nc
    mm, read, link = (c.sem(f"{name}_{s}") for s in ("product", "read", "link"))
    with nc.Block(no_gpsimd_drain=True) as block:
        if before is not None:
            block.sync(before)

        @block.tensor
        def _(pe):
            pe.wait_ge(w_in_sem, 16)
            for t in range(NT):
                for half in range(2):
                    i = 2 * t + half
                    if i >= 8:
                        pe.wait_ge(read, i - 7)
                    for q in range(KD):
                        last = nc.tensor.matmul(c.bank(i % 8), aT[:, q, P * t:P * t + P], w[:, q, BANK * half:BANK * half + BANK],
                                                start=q == 0, stop=q == KD - 1)
                    last.then_inc(mm, 1)

        @block.vector
        def _(dve):
            for t in range(NT):
                dve.wait_ge(k.tile_in[t], 16 * turn)
                for half in range(2):
                    i = 2 * t + half
                    cols = slice(BANK * half, BANK * half + BANK)
                    dve.wait_ge(mm, i + 1)
                    if gate is not None:
                        if i >= 2:
                            dve.wait_ge(link, i - 1)
                        nc.vector.tensor_tensor(k.tmp[:, BANK * (i % 2):BANK * (i % 2) + BANK], c.bank(i % 8), gate[:, cols],
                                                ALU.mult).then_inc(read, 1)
                        dve.wait_ge(read, i + 1)
                        nc.vector.tensor_tensor(out[:, t, cols], k.tmp[:, BANK * (i % 2):BANK * (i % 2) + BANK],
                                                x[:, t, cols], ALU.add).then_inc(link, 1)
                    else:
                        nc.vector.tensor_tensor(out[:, t, cols], c.bank(i % 8), x[:, t, cols], ALU.add).then_inc(read, 1)


def first_attention(c, k, d, upto=99):
    nc = c.nc
    g = lambda t: list(range(t, t + 4))
    F = k.F
    x_all = c.area("x_all", F, NK, D)
    k.hT = c.area("hT", F + 10240, KD, SEQ)
    k.hcT = c.area("hcT", F + 18432, KD, CTX)
    k.w_in = c.area("w_in", F + 20480, KD, W_IN)
    k.junk = c.area("junk", F + 32000, D)
    k.raw = c.area("raw", F + 41088, 2, 928)
    k.w_in_in = c.sem("w_in_in")
    k.w_out_in = c.sem("w_out_in")
    k.up_in = {"q": c.sem("w_q_up_in"), "kv": c.sem("w_kv_up_in")}

    def loads(sp):
        for t in range(NK):
            src = d["x"][0, P * t:P * t + P, :] if t < NT else d["ctx"][0, P * (t - NT):P * (t - NT) + P, :]
            sp.dma_start(x_all[:, t, :], src).then_inc(k.tile_in[t], 16)
        sp.dma_start(k.w_in[:, :, :], d["w_in"]).then_inc(k.w_in_in, 16)

    norm_tokens(c, "norm_a", x_all, x_all, NK, k.eps, k.junk, k.stat, loads, k.tile_in)
    groups = []
    for t0, n, dst, sc, sh in ((0, 4, k.hT, k.scale_a, 0), (4, 4, k.hT, k.scale_a, 0), (8, 2, k.hcT, k.scale_ac, 1)):
        for q in range(KD):
            at = P * (t0 % NT)
            groups.append(([x_all[:, t, P * q:P * q + P] for t in range(t0, t0 + n)], dst[:, q, at:at + P * n],
                           sc[:, q:q + 1], k.mod[:, q, sh:sh + 1]))
    transpose_groups(c, "turn_h", groups, k.ident)

    k.qk_tok = c.area("qk_tok", F, NK, 640)
    k.lat_tok = c.area("lat_tok", F + 33024, NK, 640)
    k.v_a = c.area("v_a", F + 39424, NK, 128)
    k.kr_key = c.area("kr_key", F + 40704, NK, ROPE)
    k.lstat = c.area("lstat", F + 41024, 3, NK, 2)
    project_in(c, k, d)

    k.qT_a = c.area("qT_a", F + 41088, 4, SEQ)
    k.kT_a = c.area("kT_a", F + 45184, NK * P)
    k.cqT = c.area("cqT", F + 20480, KQ, SEQ)
    k.ckvT = c.area("ckvT", F + 23552, KKV, NK * P)
    k.w_q_up = c.area("w_q_up", F + 26112, KQ, 768)
    k.w_kv_up = c.area("w_kv_up", F + 28416, KKV, 1024)
    groups = []
    for t0 in (0, 4):
        for j in range(4):
            groups.append(([k.qk_tok[:, t, P * j:P * j + P] for t in g(t0)], k.qT_a[:, j, P * t0:P * t0 + BANK], DA ** -0.5, None))
        groups.append(([k.qk_tok[:, t, 512:640] for t in g(t0)], k.kT_a[:, CTX + P * t0:CTX + P * t0 + BANK], None, None))
        for q in range(KQ):
            groups.append(([k.lat_tok[:, t, 256 + P * q:256 + P * q + P] for t in g(t0)], k.cqT[:, q, P * t0:P * t0 + BANK],
                           k.q_norm[:, q:q + 1], None))
        for q in range(KKV):
            groups.append(([k.lat_tok[:, t, P * q:P * q + P] for t in g(t0)], k.ckvT[:, q, CTX + P * t0:CTX + P * t0 + BANK],
                           k.kv_norm[:, q:q + 1], None))
    groups.append(([k.qk_tok[:, t, 512:640] for t in (8, 9)], k.kT_a[:, 0:CTX], None, None))
    for q in range(KKV):
        groups.append(([k.lat_tok[:, t, P * q:P * q + P] for t in (8, 9)], k.ckvT[:, q, 0:CTX], k.kv_norm[:, q:q + 1], None))
    transpose_groups(c, "turn_in", groups, k.ident)

    k.O = c.area("O", F, NT, D)
    prob = c.area("prob", F + 30464, 2, NK * P)
    probT = c.area("probT", F + 33024, 2, NK * P)
    st = c.area("softmax_columns", F + 35584, 8, 4)

    def up_weights(sp):
        sp.dma_start(k.w_q_up[:, :, :], d["w_q_up"]).then_inc(k.up_in["q"], 16)
        sp.dma_start(k.w_kv_up[:, :, :], d["w_kv_up"]).then_inc(k.up_in["kv"], 16)

    units = []
    for j in range(4):
        for qt in range(NT):
            for half in range(2):
                h = j + 4 * half
                rows = slice(64 * half, 64 * half + 64)
                lo, hi = max(qt - 1, 0), min(qt + 1, NT - 1)
                keys = [(0, k.kT_a[rows, 0:CTX])]
                n1 = min(2, hi - lo + 1)
                keys.append((CTX, k.kT_a[rows, CTX + P * lo:CTX + P * (lo + n1)]))
                if hi - lo + 1 > n1:
                    keys.append((CTX + P * n1, k.kT_a[rows, CTX + P * (lo + n1):CTX + P * (hi + 1)]))
                masks = []
                if lo < qt:
                    masks.append((CTX, k.mask_prev[:, :]))
                if hi > qt:
                    masks.append((CTX + P * (hi - lo), k.mask_next[:, :]))
                tiles = [0, 1] + [NC + t for t in range(lo, hi + 1)]
                units.append(Unit(k.qT_a[rows, j, P * qt:P * qt + P], keys,
                                  [k.v_a[:, t, 64 * half:64 * half + 64] for t in tiles],
                                  k.O[:, qt, 64 * h:64 * h + 64], masks, k.sink[:, h:h + 1]))
    attend(c, k, "window", units, 3, 2, (prob, probT, st), before=up_weights)

    k.b_tok = c.area("b_tok", F + 8192, NK, HB, QKB)
    k.qT_b = c.area("qT_b", F + 31232, HB, SEQ, parts=QKB)
    project_up(c, k, d, "q")
    groups = [([k.b_tok[:, t, h, :] for t in g(t0)], k.qT_b[:, h, P * t0:P * t0 + BANK], QKB ** -0.5, None)
              for t0 in (0, 4) for h in range(HB)]
    transpose_groups(c, "turn_qb", groups, k.ident)
    k.v_b = c.area("v_b", F + 15872, NK, 512)
    project_up(c, k, d, "kv")
    k.kT_b = c.area("kT_b", F + 20992, HB, NK * P, parts=QKB)
    groups = [([k.b_tok[:, t, h, :] for t in ts], k.kT_b[:, h, P * ts[0]:P * ts[0] + P * len(ts)], None, None)
              for ts in ([0, 1, 2, 3], [4, 5, 6, 7], [8, 9]) for h in range(HB)]
    transpose_groups(c, "turn_kb", groups, k.ident)
    prob = c.area("prob_b", F + 8192, 2, NK * P)
    probT = c.area("probT_b", F + 10752, 2, NK * P)
    st = c.area("softmax_columns_b", F + 13312, 8, 4)
    units = [Unit(k.qT_b[:, h, P * qt:P * qt + P], [(a, k.kT_b[:, h, a:min(a + BANK, NK * P)]) for a in range(0, NK * P, BANK)],
                  [k.v_b[:, t, 64 * h:64 * h + 64] for t in range(NK)], k.O[:, qt, 512 + 64 * h:512 + 64 * h + 64])
             for h in range(HB) for qt in range(NT)]
    attend(c, k, "latent", units, 2, 3, (prob, probT, st))

    k.OT = c.area("OT", F + 8192, KD, SEQ)
    k.w_out = c.area("w_out", F + 16384, KD, D)
    x_again = c.area("x_again", F + 24576, NT, D)
    groups = [([k.O[:, t, P * q:P * q + P] for t in g(t0)], k.OT[:, q, P * t0:P * t0 + BANK], None, None)
              for t0 in (0, 4) for q in range(KD)]
    transpose_groups(c, "turn_o", groups, k.ident)

    def out_loads(sp):
        sp.dma_start(k.w_out[:, :, :], d["w_out"]).then_inc(k.w_out_in, 16)
        for t in range(NT):
            sp.dma_start(x_again[:, t, :], d["x"][0, P * t:P * t + P, :]).then_inc(k.tile_in[t], 16)

    k.x1 = c.area("x1", F, NT, D)
    mix_out(c, k, "mix_a", k.OT, k.w_out, k.w_out_in, k.gate_a, 2, x_again, k.x1, before=out_loads)


def route(c, k, d):
    nc = c.nc
    logits, shifted, exped, soft, turned, idx, final, link, stored, zeroed = (
        c.sem(f"route_{s}") for s in ("logits", "shifted", "exped", "softmax", "turned", "indices", "final", "link", "xn_stored", "zeroed"))
    scratch = k.route
    aff, affT, vals, idxs, idxf, cols = scratch
    with nc.Block(no_gpsimd_drain=True) as block:
        @block.sync
        def _(sp):
            for t in range(NT):
                sp.dma_start(k.xn_dram[P * t:P * t + P, :], k.xn[:, t, :]).then_inc(stored, 16)
            sp.wait_ge(zeroed, 1)
            sp.dma_start(k.y_dram.rearrange("(t p) n -> p t n", p=P), k.zero[:, :].unsqueeze(1).to_broadcast([P, NT, D])).then_inc(stored, 16)
            sp.wait_ge(stored, 16 * (NT + 1))

        @block.tensor
        def _(pe):
            pe.wait_ge(k.router_in, 16)
            for t in range(NT):
                for q in range(KD):
                    last = nc.tensor.matmul(c.ps[:, NE * t:NE * t + NE], k.h2T[:, q, P * t:P * t + P], k.w_router[:, q, :],
                                            start=q == 0, stop=q == KD - 1)
            last.then_inc(logits, 1)
            pe.wait_ge(soft, 1)
            for t in range(NT):
                last = nc.tensor.transpose(c.ps[0:NE, BANK + P * t:BANK + P * t + P], aff[:, t, :], k.ident[:, :])
            last.then_inc(turned, 1)
            pe.wait_ge(idx, 1)
            nc.tensor.transpose(c.ps[:, 3 * BANK:3 * BANK + NE], vals[:, :], k.ident[0:NE, 0:NE])
            nc.tensor.transpose(c.ps[:, 3 * BANK + 64:3 * BANK + 64 + NE], idxf[:, :], k.ident[0:NE, 0:NE]).then_inc(final, 1)

        @block.scalar
        def _(act):
            act.wait_ge(shifted, 1)
            nc.scalar.activation(aff[:, :, :], aff[:, :, :], ACT.Exp).then_inc(exped, 1)

        @block.vector
        def _(dve):
            step = Chain(dve, link)
            nc.vector.memset(k.zero[:, :], 0.0).then_inc(zeroed, 1)
            dve.wait_ge(logits, 1)
            lg = c.ps[:, 0:NT * NE].rearrange("p (t e) -> p t e", e=NE)
            wide = lambda x: x.unsqueeze(2).to_broadcast([P, NT, NE])
            step(nc.vector.reduce_max(cols[:, 0, :], lg, AX.X))
            nc.vector.tensor_tensor(aff[:, :, :], lg, wide(cols[:, 0, :]), ALU.subtract).then_inc(shifted, 1)
            dve.wait_ge(exped, 1)
            step(nc.vector.reduce_sum(cols[:, 1, :], aff[:, :, :], AX.X))
            step(nc.vector.reciprocal(cols[:, 1, :], cols[:, 1, :]))
            nc.vector.tensor_tensor(aff[:, :, :], aff[:, :, :], wide(cols[:, 1, :]), ALU.mult).then_inc(soft, 1)
            dve.wait_ge(turned, 1)
            step(nc.vector.tensor_copy(affT[:, :], c.ps[0:NE, BANK:BANK + SEQ]))
            for r in range(CAP // 8):
                top = vals[:, 8 * r:8 * r + 8]
                step(nc.vector.max(top, affT[:, :]))
                step.put(nc.vector.max_index(idxs[:, 8 * r:8 * r + 8], top, affT[:, :]))
                if r < CAP // 8 - 1:
                    step(nc.vector.match_replace(affT[:, :], top, affT[:, :], -1.0))
            step.wait()
            nc.vector.tensor_copy(idxf[:, :], idxs[:, :]).then_inc(idx, 1)
            dve.wait_ge(final, 1)
            step(nc.vector.tensor_copy(k.valT[:, :], c.ps[:, 3 * BANK:3 * BANK + NE]))
            step(nc.vector.tensor_copy(k.idxT[:, :], c.ps[:, 3 * BANK + 64:3 * BANK + 64 + NE]))


def experts(c, k, d):
    nc = c.nc
    names = ("gathered0", "gathered1", "wg_in0", "wg_in1", "wd_in0", "wd_in1", "x_turned", "hidden", "h_turned", "down",
             "x_by_act", "x_by_dve", "silu", "gated", "h_out", "y_by_act", "y_by_dve", "y_free", "y_added")
    s = {n: c.sem(f"moe_{n}") for n in names}
    x, xT, act_out, h, hT, y, wg, wu, wd = k.moe

    with nc.Block(no_gpsimd_drain=True) as block:
        @block.sync
        def _(sp):
            def load(e, slot):
                sp.dma_start(wg[:, slot, :, :], d["w_gate"][e]).then_inc(s[f"wg_in{slot}"], 16)
                sp.dma_start(wu[:, slot, :, :], d["w_up"][e]).then_inc(s[f"wg_in{slot}"], 16)

            def load_down(e, slot):
                sp.dma_start(wd[:, slot, :, :], d["w_down"][e]).then_inc(s[f"wd_in{slot}"], 16)

            for e in (0, 1):
                load(e, e)
                load_down(e, e)
            with sp.Fori(1, NE // 2) as i:
                for slot in (0, 1):
                    e = i * 2 + slot
                    sp.wait_ge(s["hidden"], e - 1)
                    load(e, slot)
                    sp.wait_ge(s["down"], e - 1)
                    load_down(e, slot)

        @block.gpsimd
        def _(pool):
            def gather(e):
                nc.gpsimd.indirect_dma_start(out=x[:, e % 2, :], out_offset=None, in_=k.xn_dram,
                                             in_offset=bass.IndirectOffsetOnAxis(ap=k.idxT[:, e:e + 1], axis=0)
                                             ).then_inc(s[f"gathered{e % 2}"], 16)

            pool.sem_inc(s["y_free"], 2)
            gather(0)
            gather(1)
            for e in range(NE):
                if e + 2 < NE:
                    pool.wait_ge(s["x_turned"], e + 1)
                    gather(e + 2)
                pool.wait_ge(s["y_by_act"], e + 1)
                pool.wait_ge(s["y_by_dve"], e + 1)
                if e:
                    pool.wait_ge(s["y_added"], 16 * e)
                    pool.sem_inc(s["y_free"], 1)
                nc.gpsimd.indirect_dma_start(out=k.y_dram, out_offset=bass.IndirectOffsetOnAxis(ap=k.idxT[:, e:e + 1], axis=0),
                                             in_=y[:, e % 2, :], in_offset=None, compute_op=ALU.add).then_inc(s["y_added"], 16)
            pool.wait_ge(s["y_added"], 16 * NE)

        @block.tensor
        def _(pe):
            def turn_x(e, slot, use, first=False):
                pe.wait_ge(s[f"gathered{slot}"], use * 16)
                if not first:
                    pe.wait_ge(s["x_by_dve"], e)
                    pe.wait_ge(s["x_by_act"], e)
                for q in range(KD):
                    last = nc.tensor.transpose(c.ps[:, P * q:P * q + P], x[:, slot, P * q:P * q + P], k.ident[:, :])
                last.then_inc(s["x_turned"], 1)

            def gate_up(e, slot, use, first=False):
                pe.wait_ge(s[f"wg_in{slot}"], use * 32)
                pe.wait_ge(s["x_by_dve"], e + 1)
                pe.wait_ge(s["x_by_act"], e + 1)
                if not first:
                    pe.wait_ge(s["gated"], e)
                for b, w in ((2, wg), (3, wu)):
                    for q in range(KD):
                        last = nc.tensor.matmul(c.bank(b), xT[:, slot, q, :], w[:, slot, q, :], start=q == 0, stop=q == KD - 1)
                last.then_inc(s["hidden"], 1)

            def turn_h(e, slot):
                pe.wait_ge(s["gated"], e + 1)
                for f in range(KF):
                    last = nc.tensor.transpose(c.ps[:, 4 * BANK + P * f:4 * BANK + P * f + P], h[:, slot, P * f:P * f + P], k.ident[:, :])
                last.then_inc(s["h_turned"], 1)

            def down(e, slot, use, first=False):
                pe.wait_ge(s[f"wd_in{slot}"], use * 16)
                pe.wait_ge(s["h_out"], e + 1)
                if not first:
                    pe.wait_ge(s["y_by_dve"], e)
                    pe.wait_ge(s["y_by_act"], e)
                for half in range(2):
                    for f in range(KF):
                        last = nc.tensor.matmul(c.bank(5 + half), hT[:, slot, f, :], wd[:, slot, f, BANK * half:BANK * half + BANK],
                                                start=f == 0, stop=f == KF - 1)
                last.then_inc(s["down"], 1)

            turn_x(0, 0, 1, True)
            gate_up(0, 0, 1, True)
            turn_x(1, 1, 1)
            turn_h(0, 0)
            gate_up(1, 1, 1)
            turn_x(2, 0, 2)
            down(0, 0, 1, True)
            turn_h(1, 1)
            gate_up(2, 0, 2)
            turn_x(3, 1, 2)
            down(1, 1, 1)
            turn_h(2, 0)
            with pe.Fori(1, NE // 2 - 1) as i:
                for slot in (1, 0):
                    e = i * 2 + (1 if slot else 2)
                    use = i + (1 if slot else 2)
                    gate_up(e, slot, use)
                    turn_x(e + 1, 1 - slot, i + 2)
                    down(e - 1, 1 - slot, i + 1)
                    turn_h(e, slot)
            gate_up(NE - 1, 1, NE // 2)
            down(NE - 2, 0, NE // 2)
            turn_h(NE - 1, 1)
            down(NE - 1, 1, NE // 2)

        @block.scalar
        def _(act):
            def turned(e, slot):
                act.wait_ge(s["x_turned"], e + 1)
                for q in range(4, 8):
                    last = nc.scalar.activation(xT[:, slot, q, :], c.ps[:, P * q:P * q + P], ACT.Identity,
                                                scale=k.scale_f[:, q:q + 1], bias=k.mod[:, 16 + q, 0:1])
                last.then_inc(s["x_by_act"], 1)

            def silu(e, slot):
                act.wait_ge(s["hidden"], e + 1)
                nc.scalar.activation(act_out[:, slot, :], c.bank(2), ACT.Silu).then_inc(s["silu"], 1)

            def result(e, slot):
                act.wait_ge(s["down"], e + 1)
                act.wait_ge(s["y_free"], e + 1)
                nc.scalar.activation(y[:, slot, 0:BANK], c.bank(5), ACT.Identity, scale=k.valT[:, bass.ds(e, 1)]).then_inc(s["y_by_act"], 1)

            def hidden(e, slot):
                act.wait_ge(s["h_turned"], e + 1)
                nc.scalar.activation(hT[:, slot, :, :], c.bank(4).rearrange("p (f n) -> p f n", f=KF), ACT.Identity).then_inc(s["h_out"], 1)

            turned(0, 0)
            silu(0, 0)
            turned(1, 1)
            hidden(0, 0)
            with act.Fori(0, NE // 2 - 1) as i:
                for slot in (1, 0):
                    e = i * 2 + (1 if slot else 2)
                    silu(e, slot)
                    turned(e + 1, 1 - slot)
                    result(e - 1, 1 - slot)
                    hidden(e, slot)
            silu(NE - 1, 1)
            result(NE - 2, 0)
            hidden(NE - 1, 1)
            result(NE - 1, 1)

        @block.vector
        def _(dve):
            def turned(e, slot):
                dve.wait_ge(s["x_turned"], e + 1)
                for q in range(4):
                    last = nc.vector.tensor_scalar(xT[:, slot, q, :], c.ps[:, P * q:P * q + P], k.scale_f[:, q:q + 1],
                                                   k.mod[:, 16 + q, 0:1], ALU.mult, ALU.add)
                last.then_inc(s["x_by_dve"], 1)

            def gated(e, slot):
                dve.wait_ge(s["silu"], e + 1)
                nc.vector.tensor_tensor(h[:, slot, :], c.bank(3), act_out[:, slot, :], ALU.mult).then_inc(s["gated"], 1)

            def result(e, slot):
                dve.wait_ge(s["down"], e + 1)
                dve.wait_ge(s["y_free"], e + 1)
                nc.vector.tensor_scalar(y[:, slot, BANK:D], c.bank(6), k.valT[:, bass.ds(e, 1)], None, ALU.mult).then_inc(s["y_by_dve"], 1)

            turned(0, 0)
            gated(0, 0)
            turned(1, 1)
            with dve.Fori(0, NE // 2 - 1) as i:
                for slot in (1, 0):
                    e = i * 2 + (1 if slot else 2)
                    gated(e, slot)
                    turned(e + 1, 1 - slot)
                    result(e - 1, 1 - slot)
            gated(NE - 1, 1)
            result(NE - 2, 0)
            result(NE - 1, 1)


def add_experts(c, k, d):
    nc = c.nc
    link = c.sem("moe_add")
    with nc.Block(no_gpsimd_drain=True) as block:
        @block.sync
        def _(sp):
            for t in range(NT):
                sp.dma_start(k.xn[:, t, :], k.y_dram[P * t:P * t + P, :]).then_inc(k.tile_in[t], 16)
            sp.dma_start(k.norm_rows[:, :], d["norm_final"]).then_inc(k.norm_rows_in, 16)

        @block.vector
        def _(dve):
            step = Chain(dve, link)
            for t in range(NT):
                dve.wait_ge(k.tile_in[t], 16 * 3)
                step(nc.vector.tensor_tensor(k.xn[:, t, :], k.xn[:, t, :], k.gate_f[:, :], ALU.mult))
                nc.vector.tensor_tensor(k.x1[:, t, :], k.x1[:, t, :], k.xn[:, t, :], ALU.add)


def scale_rows(c, k, x, n, weights, arrived, count=16):
    nc = c.nc
    with nc.Block(no_gpsimd_drain=True) as block:
        @block.vector
        def _(dve):
            dve.wait_ge(arrived, count)
            for t in range(n):
                nc.vector.tensor_tensor(x[:, t, :], x[:, t, :], weights[:, :], ALU.mult)


def first_experts(c, k, d):
    nc, F = c.nc, k.F
    k.xn = c.area("xn", F + 8192, NT, D)
    k.h2T = c.area("h2T", F + 16384, KD, SEQ)
    k.junk = c.area("junk_f", F + 24576, D)
    k.w_router = c.area("w_router", F + 25600, KD, NE)
    k.route = (c.area("aff", F + 25728, NT, NE), c.area("affT", F + 25856, SEQ, parts=NE), c.area("top_vals", F + 26880, CAP, parts=NE),
               c.area("top_idx", F + 27008, CAP, dtype=U32, parts=NE), c.area("top_idx_f", F + 27136, CAP, parts=NE),
               c.area("route_cols", F + 27264, 2, NT))
    k.zero = c.area("zeros", F + 27392, D)
    k.valT = c.area("valT", F + 28416, NE)
    k.idxT = c.area("idxT", F + 28432, NE, dtype=U32)
    k.xn_dram = nc.dram_tensor("xn_rows", (SEQ, D), F32).ap()
    k.y_dram = nc.dram_tensor("expert_sums", (SEQ, D), F32).ap()
    k.router_in, k.norm_rows_in = c.sem("router_in"), c.kept_sem("norm_rows_in")

    def load_router(sp):
        sp.dma_start(k.w_router[:, :, :], d["w_router"]).then_inc(k.router_in, 16)

    norm_tokens(c, "norm_f", k.x1, k.xn, NT, k.eps, k.junk, k.stat, load_router)
    groups = [([k.xn[:, t, P * q:P * q + P] for t in range(t0, t0 + 4)], k.h2T[:, q, P * t0:P * t0 + BANK],
               k.scale_f[:, q:q + 1], k.mod[:, 16 + q, 0:1]) for t0 in (0, 4) for q in range(KD)]
    transpose_groups(c, "turn_h2", groups, k.ident)
    route(c, k, d)
    at = F + 28448
    k.moe = (c.area("expert_x", F + 8192, 2, D), c.area("expert_xT", F + 10240, 2, KD, P), c.area("expert_silu", F + 12288, 2, FF),
             c.area("expert_h", F + 13312, 2, FF), c.area("expert_hT", F + 14336, 2, KF, P), c.area("expert_y", F + 15360, 2, D),
             c.area("expert_wg", at, 2, KD, FF), c.area("expert_wu", at + 8192, 2, KD, FF), c.area("expert_wd", F + 17408, 2, KF, D))
    experts(c, k, d)
    k.norm_rows = c.area("norm_rows", F + 16384, D)
    add_experts(c, k, d)
    k.xm = k.x1
    if LAST <= 2: return
    norm_tokens(c, "norm_1", k.x1, k.x1, NT, k.eps, k.junk, k.stat)
    scale_rows(c, k, k.x1, NT, k.norm_rows, k.norm_rows_in)


def layout_experts(x, a):
    x["w_router"] = by_rows(a["w_router"][0])
    for n in ("w_gate", "w_up", "w_down"):
        w = a[n][0]
        x[n] = np.ascontiguousarray(w.reshape(NE, w.shape[1] // P, P, w.shape[2]).transpose(0, 2, 1, 3))
    x["norm_final"] = rows(a["norm_final"])


def feature_rows(c, k, name, w, w_dram, n, hT, out, taps=None, acc=None, scale=None):
    nc = c.nc
    w_in = [c.sem(f"{name}_w_in{i}") for i in range(4)]
    mm, tapped, read, out_done = (c.sem(f"{name}_{s}") for s in ("product", "tapped", "read", "out"))
    K = 4
    flat = out.rearrange("p n t -> p (n t)")

    def both(slot):
        return c.ps[:, 2 * BANK * slot:2 * BANK * slot + SEQ]

    with nc.Block(no_gpsimd_drain=True) as block:
        @block.sync
        def _(sp):
            for slot in range(4):
                sp.dma_start(w[:, slot, :, :], w_dram[slot]).then_inc(w_in[slot], 16)
            with sp.Fori(1, n // 4) as i:
                for slot in range(4):
                    sp.wait_ge(mm, i * 4 + (slot - 3))
                    sp.dma_start(w[:, slot, :, :], w_dram[i * 4 + slot]).then_inc(w_in[slot], 16)

        @block.tensor
        def _(pe):
            with pe.Fori(0, n // 4) as i:
                for slot in range(4):
                    pe.wait_ge(w_in[slot], i * 16 + 16)
                    pe.wait_ge(read, i * 4 + (slot + 1))
                    for half in range(2):
                        for q in range(KD):
                            last = nc.tensor.matmul(both(slot)[:, BANK * half:BANK * half + BANK], w[:, slot, q, :],
                                                    hT[:, q, BANK * half:BANK * half + BANK], start=q == 0, stop=q == KD - 1)
                    last.then_inc(mm, 1)

        if taps is None:
            @block.scalar
            def _(act):
                act.sem_inc(read, 4)
                with act.Fori(0, n // 4) as i:
                    for slot in range(4):
                        act.wait_ge(mm, i * 4 + (slot + 1))
                        nc.scalar.activation(flat[:, bass.ds((i * 4 + slot) * SEQ, SEQ)], both(slot), ACT.Identity,
                                             scale=scale[:, bass.ds(i * 4 + slot, 1)]).then_inc(read, 1)
        else:
            @block.scalar
            def _(act):
                with act.Fori(0, n // 4) as i:
                    for slot in range(4):
                        f = i * 4 + slot
                        act.wait_ge(mm, f + 1)
                        nc.scalar.activation(acc[:, slot % 2, :], both(slot), ACT.Identity,
                                             scale=taps[:, bass.ds(f * K + (K - 1), 1)]).then_inc(tapped, 1)
                        act.wait_ge(out_done, f * (K - 1) + (K - 1))
                        nc.scalar.activation(flat[:, bass.ds(f * SEQ, SEQ)], acc[:, slot % 2, :], ACT.Silu)

            @block.vector
            def _(dve):
                dve.sem_inc(read, 4)
                with dve.Fori(0, n // 4) as i:
                    for slot in range(4):
                        f = i * 4 + slot
                        dve.wait_ge(tapped, f + 1)
                        for j in range(1, K):
                            if j > 1:
                                dve.wait_ge(out_done, f * (K - 1) + (j - 1))
                            nc.vector.scalar_tensor_tensor(acc[:, slot % 2, j:SEQ], both(slot)[:, 0:SEQ - j],
                                                           taps[:, bass.ds(f * K + (K - 1 - j), 1)], acc[:, slot % 2, j:SEQ],
                                                           ALU.mult, ALU.add).then_inc(out_done, 1)
                        dve.wait_ge(out_done, f * (K - 1) + (K - 1))
                        dve.sem_inc(read, 1)


def token_rows(c, k, name, hT, w, w_sem, width, finish):
    nc = c.nc
    mm, read = c.sem(f"{name}_product"), c.sem(f"{name}_read")
    with nc.Block(no_gpsimd_drain=True) as block:
        @block.tensor
        def _(pe):
            pe.wait_ge(w_sem, 16)
            for t in range(NT):
                if t >= 4:
                    pe.wait_ge(read, t - 3)
                for a in range(0, width, BANK):
                    b = min(a + BANK, width)
                    for q in range(KD):
                        last = nc.tensor.matmul(c.ps[:, 2 * BANK * (t % 4) + a:2 * BANK * (t % 4) + b], hT[:, q, P * t:P * t + P],
                                                w[:, q, a:b], start=q == 0, stop=q == KD - 1)
                last.then_inc(mm, 1)

        @block.scalar
        def _(act):
            for t in range(NT):
                act.wait_ge(mm, t + 1)
                finish(act, t, c.ps[:, 2 * BANK * (t % 4):2 * BANK * (t % 4) + width]).then_inc(read, 1)


def unit_rows(c, k, qkT, n, sq, root):
    nc = c.nc
    squared, summed, rooted, link, scaled = (c.sem(f"unit_{s}") for s in ("squared", "summed", "rooted", "link", "scaled"))
    with nc.Block(no_gpsimd_drain=True) as block:
        @block.scalar
        def _(act):
            def root_of(f):
                act.wait_ge(summed, f + 1)
                if f >= 2:
                    act.wait_ge(scaled, f - 1)
                s = float(GDK) if f < GH else 1.0
                nc.scalar.activation(root[:, f % 2, :], c.ps[:, SEQ * (f % 4):SEQ * (f % 4) + SEQ], ACT.Sqrt, scale=s,
                                     bias=(k.eps_q if f < GH else k.eps)[:, 0:1]).then_inc(rooted, 1)

            for f in range(n):
                if f >= 2:
                    act.wait_ge(summed, f - 1)
                nc.scalar.activation(sq[:, f % 2, :], qkT[:, f, :], ACT.Square).then_inc(squared, 1)
                if f:
                    root_of(f - 1)
            root_of(n - 1)

        @block.tensor
        def _(pe):
            for f in range(n):
                pe.wait_ge(squared, f + 1)
                if f >= 4:
                    pe.wait_ge(rooted, f - 3)
                for half in range(2):
                    at = SEQ * (f % 4) + BANK * half
                    last = nc.tensor.matmul(c.ps[:, at:at + BANK], k.ones[:, :], sq[:, f % 2, BANK * half:BANK * half + BANK],
                                            start=True, stop=True)
                last.then_inc(summed, 1)

        @block.vector
        def _(dve):
            step = Chain(dve, link)
            for f in range(n):
                dve.wait_ge(rooted, f + 1)
                step(nc.vector.reciprocal(root[:, f % 2, :], root[:, f % 2, :]))
                nc.vector.tensor_tensor(qkT[:, f, :], qkT[:, f, :], root[:, f % 2, :], ALU.mult).then_inc(scaled, 1)


def delta_gates(c, k, ba):
    nc = c.nc
    a1, e1, l1, g1, s1, r1, link, x1 = (c.sem(f"gates_{s}") for s in ("linear", "exp", "log", "gate", "sums", "read", "link", "decays"))
    G = k.gates
    T = NT * GH
    with nc.Block(no_gpsimd_drain=True) as block:
        @block.vector
        def _(dve):
            step = Chain(dve, link)
            dve.wait_ge(k.second_in, 16 * k.n_second)
            lin = ba.rearrange("p t n -> p n t")
            bc = lambda x: x.unsqueeze(1).to_broadcast([P, NT, GH])
            v = lambda r: G[:, r, :].rearrange("p (t h) -> p t h", h=GH)
            step.put(nc.vector.tensor_copy(v(0), ba[:, :, 0:GH]))
            step(nc.vector.tensor_tensor(v(6), ba[:, :, GH:2 * GH], bc(k.dt_bias[:, :]), ALU.add))
            step.put(nc.vector.tensor_scalar(G[:, 7, :], G[:, 6, :], -1.0, None, ALU.mult))
            step.put(nc.vector.tensor_scalar(G[:, 1, :], G[:, 6, :], 0.0, None, ALU.max))
            step.wait()
            nc.vector.tensor_tensor(G[:, 8, :], G[:, 7, :], G[:, 6, :], ALU.min).then_inc(a1, 1)
            dve.wait_ge(l1, 1)
            step(nc.vector.tensor_tensor(G[:, 1, :], G[:, 1, :], G[:, 8, :], ALU.add))
            step(nc.vector.scalar_tensor_tensor(v(1), v(1), -1.0, bc(k.a_exp[:, :]), ALU.mult, ALU.mult))
            dve.sem_inc(g1, 1)
            dve.wait_ge(s1, 1)
            step.put(nc.vector.tensor_scalar(G[:, 2, :], c.ps[:, 0:T], -1.0, None, ALU.mult))
            step.put(nc.vector.tensor_copy(G[:, 6, :], c.ps[:, 0:T]))
            step.wait()
            nc.vector.tensor_tensor(G[:, 7, :], c.ps[:, T:2 * T], G[:, 2, :], ALU.add).then_inc(r1, 1)
            dve.wait_ge(r1, 1)
            nc.vector.tensor_copy(k.chunk_decay[:, :, :], c.ps[:, 2 * T:4 * T].rearrange("p (r n) -> p r n", r=2)).then_inc(r1, 1)
            dve.wait_ge(x1, 1)
            nc.vector.tensor_tensor(G[:, 5, :], G[:, 0, :], G[:, 3, :], ALU.mult)

        @block.scalar
        def _(act):
            act.wait_ge(k.second_in, 16 * k.n_second)
            act.wait_ge(a1, 1)
            nc.scalar.activation(G[:, 0, :], G[:, 0, :], ACT.Sigmoid)
            nc.scalar.activation(k.a_exp[:, :], k.a_log[:, :], ACT.Exp)
            nc.scalar.activation(G[:, 8, :], G[:, 8, :], ACT.Exp).then_inc(e1, 1)
            act.wait_ge(e1, 1)
            nc.scalar.activation(G[:, 8, :], G[:, 8, :], ACT.Ln, bias=k.ones[:, 0:1]).then_inc(l1, 1)
            act.wait_ge(r1, 2)
            nc.scalar.activation(G[:, 4, :], G[:, 7, :], ACT.Exp)
            nc.scalar.activation(k.chunk_decay[:, :, :], k.chunk_decay[:, :, :], ACT.Exp)
            nc.scalar.activation(G[:, 3, :], G[:, 6, :], ACT.Exp).then_inc(x1, 1)

        @block.tensor
        def _(pe):
            pe.wait_ge(g1, 1)
            for i, lhsT in enumerate((k.tri, k.same, k.first_half, k.second_half)):
                last = nc.tensor.matmul(c.ps[:, T * i:T * i + T], lhsT[:, :], G[:, 1, :], start=True, stop=True)
            last.then_inc(s1, 1)


def delta_rows(c, k, ktok, kb, vtok):
    nc = c.nc
    link = c.sem("delta_rows")
    v = lambda r, t: k.gates[:, r, GH * t:GH * t + GH].unsqueeze(2).to_broadcast([P, GH, P])
    with nc.Block(no_gpsimd_drain=True) as block:
        @block.vector
        def _(dve):
            for t in range(NT):
                nc.vector.tensor_tensor(kb[:, t], ktok[:, t], v(0, t), ALU.mult)
                nc.vector.tensor_tensor(vtok[:, t], vtok[:, t], v(0, t), ALU.mult)


def delta_rows2(c, k, ktok, kb):
    nc = c.nc
    link = c.sem("delta_rows2")
    v = lambda r, t: k.gates[:, r, GH * t:GH * t + GH].unsqueeze(2).to_broadcast([P, GH, P])
    with nc.Block(no_gpsimd_drain=True) as block:
        @block.vector
        def _(dve):
            for t in range(NT):
                nc.vector.tensor_tensor(kb[:, t], ktok[:, t], v(5, t), ALU.mult).then_inc(link, 1)
                dve.wait_ge(link, t + 1)
                nc.vector.tensor_tensor(ktok[:, t], ktok[:, t], v(4, t), ALU.mult)


def delta_inverse(c, k, qT, kT, kbT, kbg, vb, PT, UV, WT, w):
    nc = c.nc
    spread, made, exps, at, masked, one, base, t1, t1_out, z, sub, fin, uv_out, wt_out = (
        c.sem(f"inv_{s}") for s in ("spread", "made", "decay", "rows", "masked", "first", "base", "t1", "t1_out", "z", "sub", "final", "uv_out", "wt_out"))
    gtri, E, LT, Lm, U, X, T = w
    LV = 6

    def bank(t, b):
        return c.bank(4 * (t % 2) + b)

    def hd(x):
        return x.rearrange("p (h n) -> p h n", h=GH)

    def at_level(t, l):
        return (t // 2) * 2 * (LV - 1) + (l - 1) * 2 + t % 2

    pairs = [(a, a + 1) for a in range(0, NT, 2)]
    with nc.Block(no_gpsimd_drain=True) as block:
        @block.gpsimd
        def _(pool):
            for t in range(NT):
                pool.wait_ge(at, 2 * t + 1)
                if t >= 2:
                    pool.wait_ge(fin, t - 1)
                for l in range(LV):
                    nc.gpsimd.tensor_tensor(hd(Lm[:, t % 2, l, :]), hd(LT[:, t % 2, :]),
                                            k.level[:, l, :].unsqueeze(1).to_broadcast([P, GH, P]), ALU.mult).then_inc(masked, 1)
            pool.wait_ge(masked, LV * NT)

        @block.tensor
        def _(pe):
            for pair in pairs:
                for t in pair:
                    pe.wait_ge(spread, t + 1)
                    if t >= 2:
                        pe.wait_ge(wt_out, t - 1)
                        pe.wait_ge(uv_out, t - 1)
                    nc.tensor.matmul(bank(t, 0), k.ones[:, :], gtri[:, t % 2, :], start=True, stop=False)
                    nc.tensor.matmul(bank(t, 0), k.ident_bf[:, :], k.mask_up[:, :], start=False, stop=True)
                    for b, other in ((1, kbT), (2, qT)):
                        for h in range(GH):
                            last = nc.tensor.matmul(bank(t, b)[:, P * h:P * h + P], kT[:, h, P * t:P * t + P],
                                                    other[:, h, P * t:P * t + P], start=True, stop=True)
                    last.then_inc(made, 1)
                for t in pair:
                    pe.wait_ge(masked, LV * t + 1)
                    for h in range(GH):
                        last = nc.tensor.matmul(bank(t, 3)[:, P * h:P * h + P], Lm[:, t % 2, 0, P * h:P * h + P], k.ident[:, :],
                                                start=True, stop=True)
                    last.then_inc(one, 1)
                for l in range(1, LV):
                    for t in pair:
                        pe.wait_ge(masked, LV * t + l + 1)
                        if l == 1:
                            pe.wait_ge(base, t + 1)
                        else:
                            pe.wait_ge(sub, at_level(t, l - 1) + 1)
                        for h in range(GH):
                            last = nc.tensor.matmul(bank(t, 0)[:, P * h:P * h + P], Lm[:, t % 2, l, P * h:P * h + P],
                                                    X[:, t % 2, P * h:P * h + P], start=True, stop=True)
                        last.then_inc(t1, 1)
                    for t in pair:
                        pe.wait_ge(t1_out, at_level(t, l) + 1)
                        for h in range(GH):
                            last = nc.tensor.matmul(bank(t, 1)[:, P * h:P * h + P], T[:, t % 2, P * h:P * h + P],
                                                    U[:, t % 2, P * h:P * h + P], start=True, stop=True)
                        if l < LV - 1:
                            for h in range(GH):
                                last = nc.tensor.matmul(bank(t, 2)[:, P * h:P * h + P], U[:, t % 2, P * h:P * h + P],
                                                        T[:, t % 2, P * h:P * h + P], start=True, stop=True)
                        last.then_inc(z, 1)
                for t in pair:
                    pe.wait_ge(sub, at_level(t, LV - 1) + 1)
                    for h in range(GH):
                        nc.tensor.matmul(bank(t, 3)[:, P * h:P * h + P], U[:, t % 2, P * h:P * h + P], vb[:, t, h, :],
                                         start=True, stop=True)
                    for h in range(GH):
                        last = nc.tensor.matmul(bank(t, 0)[:, P * h:P * h + P], kbg[:, t, h, :], U[:, t % 2, P * h:P * h + P],
                                                start=True, stop=True)
                    last.then_inc(fin, 1)

        @block.scalar
        def _(act):
            for pair in pairs:
                for t in pair:
                    act.wait_ge(made, t + 1)
                    if t >= 2:
                        act.wait_ge(at, 2 * (t - 1))
                    for h in range(GH):
                        last = nc.scalar.activation(E[:, t % 2, P * h:P * h + P], bank(t, 0)[:, P * h:P * h + P], ACT.Exp,
                                                    bias=k.gates[:, 2, GH * t + h:GH * t + h + 1])
                    last.then_inc(exps, 1)
                for l in range(1, LV):
                    for t in pair:
                        act.wait_ge(t1, at_level(t, l) + 1)
                        nc.scalar.activation(T[:, t % 2, :], bank(t, 0), ACT.Identity).then_inc(t1_out, 1)
                for t in pair:
                    act.wait_ge(fin, t + 1)
                    nc.scalar.activation(UV[:, t], hd(bank(t, 3)), ACT.Identity).then_inc(uv_out, 1)

        @block.vector
        def _(dve):
            for pair in pairs:
                for t in pair:
                    if t >= 2:
                        dve.wait_ge(made, t - 1)
                    nc.vector.tensor_tensor(hd(gtri[:, t % 2, :]), k.tri[:, :].unsqueeze(1).to_broadcast([P, GH, P]),
                                            k.gates[:, 1, GH * t:GH * t + GH].unsqueeze(2).to_broadcast([P, GH, P]),
                                            ALU.mult).then_inc(spread, 1)
                for t in pair:
                    dve.wait_ge(exps, t + 1)
                    if t >= 2:
                        dve.wait_ge(masked, LV * (t - 1))
                    nc.vector.tensor_tensor(LT[:, t % 2, :], bank(t, 1), E[:, t % 2, :], ALU.mult).then_inc(at, 1)
                    nc.vector.tensor_tensor(PT[:, t], hd(bank(t, 2)), hd(E[:, t % 2, :]), ALU.mult).then_inc(at, 1)
                wide = k.ident[:, :].unsqueeze(1).to_broadcast([P, GH, P])
                for t in pair:
                    dve.wait_ge(one, t + 1)
                    nc.vector.tensor_tensor(hd(X[:, t % 2, :]), wide, hd(bank(t, 3)), ALU.subtract)
                    nc.vector.tensor_tensor(hd(U[:, t % 2, :]), wide, hd(Lm[:, t % 2, 0, :]), ALU.subtract).then_inc(base, 1)
                for l in range(1, LV):
                    for t in pair:
                        dve.wait_ge(z, at_level(t, l) + 1)
                        if l < LV - 1:
                            nc.vector.tensor_tensor(X[:, t % 2, :], X[:, t % 2, :], bank(t, 2), ALU.subtract)
                        nc.vector.tensor_tensor(U[:, t % 2, :], U[:, t % 2, :], bank(t, 1), ALU.subtract).then_inc(sub, 1)
                for t in pair:
                    dve.wait_ge(fin, t + 1)
                    nc.vector.tensor_copy(WT[:, t], hd(bank(t, 0))).then_inc(wt_out, 1)


def delta_scan(c, k, qT, kd, PT, UV, WT, S, Sg, Us, o, tq):
    nc = c.nc
    ws, us, ku, st, sg, ot, link, qs = (c.sem(f"scan_{s}") for s in ("ws", "u", "ku", "state", "decayed", "out", "link", "qs"))
    N = SEQ // CHUNK
    with nc.Block(no_gpsimd_drain=True) as block:
        @block.tensor
        def _(pe):
            for n in range(N):
                t, r = n // 2, n % 2
                rows = slice(CHUNK * r, CHUNK * r + CHUNK)
                pe.wait_ge(st, n + 1)
                for h in range(GH):
                    last = nc.tensor.matmul(c.ps[rows, P * h:P * h + P], WT[:, t, h, rows], S[:, P * h:P * h + P], start=True, stop=True)
                last.then_inc(ws, 1)
                if n:
                    pe.wait_ge(ot, 2 * n)
                for h in range(GH):
                    last = nc.tensor.matmul(c.ps[rows, BANK + P * h:BANK + P * h + P], qT[:, h, CHUNK * n:CHUNK * n + CHUNK],
                                            S[:, P * h:P * h + P], start=True, stop=True)
                last.then_inc(qs, 1)
                pe.wait_ge(us, n + 1)
                for h in range(GH):
                    last = nc.tensor.matmul(c.bank(2)[:, P * h:P * h + P], kd[rows, t, h, :], Us[rows, P * h:P * h + P], start=True, stop=True)
                last.then_inc(ku, 1)
                for h in range(GH):
                    last = nc.tensor.matmul(c.ps[rows, 3 * BANK + P * h:3 * BANK + P * h + P], PT[rows, t, h, rows],
                                            Us[rows, P * h:P * h + P], start=True, stop=True)
                last.then_inc(link, 1)

        @block.gpsimd
        def _(pool):
            for n in range(N):
                t, r = n // 2, n % 2
                pool.wait_ge(st, n + 1)
                if n:
                    pool.wait_ge(ku, n)
                d = k.chunk_decay[:, r, GH * t:GH * t + GH].unsqueeze(2).to_broadcast([P, GH, P])
                nc.gpsimd.tensor_tensor(Sg[:, :].rearrange("p (h n) -> p h n", h=GH), S[:, :].rearrange("p (h n) -> p h n", h=GH), d,
                                        ALU.mult).then_inc(sg, 1)

        @block.vector
        def _(dve):
            hd = lambda x: x.rearrange("p (h n) -> p h n", h=GH)
            nc.vector.memset(S[:, :], 0.0).then_inc(st, 1)
            for n in range(N):
                t, r = n // 2, n % 2
                rows = slice(CHUNK * r, CHUNK * r + CHUNK)
                dve.wait_ge(ws, n + 1)
                nc.vector.tensor_tensor(hd(Us[rows, :]), UV[rows, t], hd(c.ps[rows, 0:BANK]), ALU.subtract).then_inc(us, 1)
                dve.wait_ge(qs, n + 1)
                g = k.gates[rows, 3, GH * t:GH * t + GH].unsqueeze(2).to_broadcast([CHUNK, GH, P])
                nc.vector.tensor_tensor(hd(tq[rows, :]), hd(c.ps[rows, BANK:2 * BANK]), g, ALU.mult).then_inc(ot, 1)
                dve.wait_ge(sg, n + 1)
                dve.wait_ge(ku, n + 1)
                nc.vector.tensor_tensor(S[:, :], Sg[:, :], c.bank(2), ALU.add).then_inc(st, 1)
                dve.wait_ge(link, n + 1)
                dve.wait_ge(ot, 2 * n + 1)
                nc.vector.tensor_tensor(o[rows, t], hd(tq[rows, :]), hd(c.ps[rows, 3 * BANK:4 * BANK]), ALU.add).then_inc(ot, 1)


def gated_norm(c, k, o, z, tmp, cols):
    nc = c.nc
    sums, rooted, link = (c.sem(f"gnorm_{s}") for s in ("sums", "root", "link"))
    T = NT * GH
    with nc.Block(no_gpsimd_drain=True) as block:
        @block.vector
        def _(dve):
            step = Chain(dve, link)
            for t in range(NT):
                step(nc.vector.tensor_tensor(tmp[:, t % 2, :], o[:, t].rearrange("p h n -> p (h n)"), o[:, t].rearrange("p h n -> p (h n)"), ALU.mult))
                step.put(nc.vector.reduce_sum(cols[:, 0, GH * t:GH * t + GH], tmp[:, t % 2, :].rearrange("p (h n) -> p h n", h=GH), AX.X))
                step.put(nc.vector.tensor_tensor(z[:, t], z[:, t], k.gdn_norm[:, :].unsqueeze(1).to_broadcast([P, GH, P]), ALU.mult))
            step.wait()
            dve.sem_inc(sums, 1)
            dve.wait_ge(rooted, 1)
            step(nc.vector.reciprocal(cols[:, 0, :], cols[:, 1, :]))
            for t in range(NT):
                step(nc.vector.tensor_tensor(o[:, t], o[:, t], cols[:, 0, GH * t:GH * t + GH].unsqueeze(2).to_broadcast([P, GH, P]), ALU.mult))
                nc.vector.tensor_tensor(o[:, t], o[:, t], z[:, t], ALU.mult)

        @block.scalar
        def _(act):
            act.wait_ge(sums, 1)
            nc.scalar.activation(cols[:, 1, :], cols[:, 0, :], ACT.Sqrt, scale=1.0 / GDK, bias=k.eps[:, 0:1]).then_inc(rooted, 1)


def mix_branches(c, k, d, hT, aT, bT, wg, wa, wb, sig):
    nc = c.nc
    mm, sg, mul, out_s = (c.sem(f"branch_{s}") for s in ("product", "sigmoid", "scaled", "out"))
    with nc.Block(no_gpsimd_drain=True) as block:
        @block.sync
        def _(sp):
            for dst, src, s in k.branch_loads:
                sp.dma_start(dst, src).then_inc(s, 16)

        @block.tensor
        def _(pe):
            for s in k.branch_in:
                pe.wait_ge(s, 16)
            for t in range(NT):
                for half in range(2):
                    i = 2 * t + half
                    if i >= 2:
                        pe.wait_ge(mul, 2 * (i - 1))
                    cols = slice(BANK * half, BANK * half + BANK)
                    for b, (x, w, n) in enumerate(((hT, wg[0], KD), (hT, wg[1], KD), (aT, wa, 4), (bT, wb, 4))):
                        for q in range(n):
                            last = nc.tensor.matmul(c.bank(4 * half + b), x[:, q, P * t:P * t + P], w[:, q, cols], start=q == 0, stop=q == n - 1)
                    last.then_inc(mm, 1)

        @block.scalar
        def _(act):
            for i in range(2 * NT):
                act.wait_ge(mm, i + 1)
                if i >= 2:
                    act.wait_ge(out_s, i - 1)
                nc.scalar.activation(sig[:, i % 2, :], c.ps[:, 4 * BANK * (i % 2):4 * BANK * (i % 2) + 2 * BANK], ACT.Sigmoid).then_inc(sg, 1)

        @block.vector
        def _(dve):
            for t in range(NT):
                for half in range(2):
                    i = 2 * t + half
                    dve.wait_ge(sg, i + 1)
                    for b in range(2):
                        at = BANK * (4 * half + 2 + b)
                        nc.vector.tensor_tensor(sig[:, half, BANK * b:BANK * b + BANK], sig[:, half, BANK * b:BANK * b + BANK],
                                                c.ps[:, at:at + BANK], ALU.mult).then_inc(mul, 1)
                dve.wait_ge(mul, 4 * (t + 1))
                for half in range(2):
                    v = lambda b: sig[:, half, BANK * b:BANK * b + BANK].rearrange("p (q n) -> p q n", q=4)
                    nc.vector.tensor_tensor(hT[:, 4 * half:4 * half + 4, P * t:P * t + P], v(0), v(1), ALU.add).then_inc(out_s, 1)


def ffn_up(c, k, d, hT, w, actT, acc):
    nc = c.nc
    w_in = [c.sem(f"ffn_w_in{i}") for i in range(2)]
    mm, tapped, conv, silu, done = (c.sem(f"ffn_{s}") for s in ("product", "tapped", "convolved", "silu", "done"))
    K = 3
    flat = actT.rearrange("p n t -> p (n t)")

    def rows(slot, g):
        return c.ps[:, 4 * BANK * slot + SEQ * g:4 * BANK * slot + SEQ * g + SEQ]

    with nc.Block(no_gpsimd_drain=True) as block:
        @block.sync
        def _(sp):
            for slot in range(2):
                sp.dma_start(w[:, slot, :, :], d["w_ffn"][slot]).then_inc(w_in[slot], 16)
            with sp.Fori(1, NF2 // 2) as i:
                for slot in range(2):
                    sp.wait_ge(mm, i * 2 + (slot - 1))
                    sp.dma_start(w[:, slot, :, :], d["w_ffn"][i * 2 + slot]).then_inc(w_in[slot], 16)

        @block.tensor
        def _(pe):
            with pe.Fori(0, NF2 // 2) as i:
                for slot in range(2):
                    f = i * 2 + slot
                    pe.wait_ge(w_in[slot], i * 16 + 16)
                    pe.wait_ge(conv, f * 4 + 4)
                    for g in range(2):
                        for half in range(2):
                            for q in range(KD):
                                last = nc.tensor.matmul(rows(slot, g)[:, BANK * half:BANK * half + BANK], w[:, slot, KD * g + q, :],
                                                        hT[:, q, BANK * half:BANK * half + BANK], start=q == 0, stop=q == KD - 1)
                    last.then_inc(mm, 1)

        @block.scalar
        def _(act):
            with act.Fori(0, NF2 // 2) as i:
                for slot in range(2):
                    f = i * 2 + slot
                    act.wait_ge(mm, f + 1)
                    act.wait_ge(done, f + 1)
                    for g in range(2):
                        nc.scalar.activation(acc[:, slot, g, :], rows(slot, g), ACT.Identity,
                                             scale=k.ffn_taps[:, bass.ds((f * 2 + g) * 4 + 2, 1)],
                                             bias=k.ffn_taps[:, bass.ds((f * 2 + g) * 4 + 3, 1)]).then_inc(tapped, 1)
                    act.wait_ge(conv, f * 4 + 10)
                    nc.scalar.activation(acc[:, slot, 0, :], acc[:, slot, 0, :], ACT.Silu).then_inc(silu, 1)

        @block.vector
        def _(dve):
            dve.sem_inc(conv, 8)
            dve.sem_inc(done, 2)
            with dve.Fori(0, NF2 // 2) as i:
                for slot in range(2):
                    f = i * 2 + slot
                    for g in range(2):
                        dve.wait_ge(tapped, f * 2 + (g + 1))
                        for j in (1, 2):
                            if j == 2:
                                dve.wait_ge(conv, f * 4 + (8 + 2 * g + 1))
                            nc.vector.scalar_tensor_tensor(acc[:, slot, g, j:SEQ], rows(slot, g)[:, 0:SEQ - j],
                                                           k.ffn_taps[:, bass.ds((f * 2 + g) * 4 + (2 - j), 1)],
                                                           acc[:, slot, g, j:SEQ], ALU.mult, ALU.add).then_inc(conv, 1)
                    dve.wait_ge(silu, f + 1)
                    dve.wait_ge(conv, f * 4 + 12)
                    nc.vector.tensor_tensor(flat[:, bass.ds(f * SEQ, SEQ)], acc[:, slot, 0, :], acc[:, slot, 1, :], ALU.mult).then_inc(done, 1)


def ffn_down(c, k, d, actT, w, x):
    nc = c.nc
    mm, read, used = c.sem("down_product"), c.sem("down_read"), c.sem("down_used")
    w_in = [c.sem(f"down_w_in{i}") for i in range(4)]
    N = NF2 // 2
    with nc.Block(no_gpsimd_drain=True) as block:
        @block.sync
        def _(sp):
            for i in range(2 * N):
                j = i - 4
                if j >= 0 and j % N == N - 1:
                    sp.wait_ge(mm, NT * (j // N + 1))
                elif j >= 0:
                    sp.wait_ge(used, j + 1 - j // N)
                sp.dma_start(w[:, i % 4, :, :], d["w_down_2"][i // N, i % N]).then_inc(w_in[i % 4], 16)
                if 4 <= i < 4 + NT:
                    t = i - 4
                    sp.dma_start(x[:, t, :], k.x_dram[P * t:P * t + P, :]).then_inc(k.tile_in[t], 16)
            sp.dma_start(k.norm_rows2[:, :], d["norm_final_2"]).then_inc(k.norm_rows_in, 16)

        @block.tensor
        def _(pe):
            for i in range(2 * N):
                half, g = i // N, i % N
                pe.wait_ge(w_in[i % 4], 16 * (i // 4 + 1))
                for j in range(2):
                    for t in range(NT):
                        if half and g == 0 and j == 0:
                            pe.wait_ge(read, t + 1)
                        last = nc.tensor.matmul(c.bank(t), actT[:, 2 * g + j, P * t:P * t + P], w[:, i % 4, j, :],
                                                start=g == 0 and j == 0, stop=g == N - 1 and j == 1)
                        if g == N - 1 and j == 1 and t < NT - 1:
                            last.then_inc(mm, 1)
                if g == N - 1:
                    last.then_inc(mm, 1)
                else:
                    last.then_inc(used, 1)

        @block.vector
        def _(dve):
            for i in range(2 * NT):
                t, half = i % NT, i // NT
                if half == 0:
                    dve.wait_ge(k.tile_in[t], 16 * k.turn_down)
                dve.wait_ge(mm, i + 1)
                cols = slice(BANK * half, BANK * half + BANK)
                nc.vector.tensor_tensor(x[:, t, cols], x[:, t, cols], c.bank(t), ALU.add).then_inc(read, 1)


def store_rows(c, name, pairs):
    stored = c.sem(f"{name}_stored")
    with c.nc.Block(no_gpsimd_drain=True) as block:
        @block.sync
        def _(sp):
            for dst, src in pairs:
                sp.dma_start(dst, src).then_inc(stored, 16)
            sp.wait_ge(stored, 16 * len(pairs))


def load_all(c, loads):
    with c.nc.Block(no_gpsimd_drain=True) as block:
        @block.sync
        def _(sp):
            for dst, src, s in loads:
                sp.dma_start(dst, src).then_inc(s, 16)


def second_block(c, k, d, out):
    nc = c.nc
    at = [k.F2]

    def put(name, *shape, dtype=F32):
        n = int(np.prod(shape)) * (2 if dtype == BF16 else 4) // 4
        t = c.area("s_" + name, at[0], *shape, dtype=dtype)
        at[0] += -(-n // 8) * 8
        return t

    loads = []

    def loaded(name, *shape, dtype=F32):
        t = put(name, *shape, dtype=dtype)
        loads.append((t[:], d[name]))
        return t

    k.tri, k.same, k.first_half, k.second_half = (loaded(n, P) for n in ("tri", "same", "first_half", "second_half"))
    k.mask_up, k.level = loaded("mask_up", GH * P, dtype=BF16), loaded("level", 6, P)
    k.norm_mix, k.norm_ffn2 = loaded("norm_mix", KD), loaded("norm_ffn2", KD)
    k.conv_taps, k.ffn_taps = loaded("conv_taps", 12 * 4), loaded("ffn_taps", 2 * NF2 * 4)
    k.dt_bias, k.a_log, k.gdn_norm, k.qb_scale = loaded("dt_bias", GH), loaded("a_log", GH), loaded("gdn_norm", GDK), loaded("qb_scale", 8)
    k.ones, k.eps_q, k.a_exp = put("ones", P), put("eps_q", 1), put("a_exp", GH)
    k.gates, k.chunk_decay = put("gates", 9, NT * GH), put("chunk_decay", 2, NT * GH)
    k.ba, k.cols = put("ba", NT, 2 * GH), put("cols", 2, NT * GH)
    k.second_in, k.n_second = c.sem("second_in"), len(loads)
    A = at[0]
    assert A <= k.F
    x2 = k.x1
    k.x_dram = nc.dram_tensor("x_rows", (SEQ, D), F32).ap()
    hT_dram = nc.dram_tensor("h_rows", (P, KD, SEQ), F32).ap()
    store_rows(c, "x2", [(k.x_dram[P * t:P * t + P, :], x2[:, t, :]) for t in range(NT)])
    top = c.words - NT * D
    xn = c.area("xn2", top, NT, D)
    k.junk = c.area("junk2", top - D, D)
    norm_tokens(c, "norm_2", x2, xn, NT, k.eps, k.junk, k.stat)

    with nc.Block(no_gpsimd_drain=True) as block:
        @block.sync
        def _(sp):
            for dst, src in loads:
                sp.dma_start(dst, src).then_inc(k.second_in, 16)

        @block.vector
        def _(dve):
            nc.vector.memset(k.ones[:, :], 1.0)
            nc.vector.memset(k.eps_q[:, :], EPS * GDK)
            dve.wait_ge(k.second_in, 16 * len(loads))

    hT = c.area("hT2", A, KD, SEQ)
    M = A + 8192
    g4 = lambda t: list(range(t, t + 4))
    groups = [([xn[:, t, P * q:P * q + P] for t in g4(t0)], hT[:, q, P * t0:P * t0 + BANK], k.norm_mix[:, q:q + 1], None)
              for t0 in (0, 4) for q in range(KD)]
    transpose_groups(c, "turn_h3", groups, k.ident)

    feat = c.area("featT", M, 12, SEQ)
    ring = c.area("feat_ring", M + 12288, 4, KD, P)
    acc = c.area("feat_acc", M + 16384, 2, SEQ)
    feature_rows(c, k, "delta_feat", ring, d["w_feat"], 12, hT, feat[:, :, :], k.conv_taps, acc)
    w_z = c.area("w_z", M + 12288, KD, 520)
    z = c.area("z_tok", M + 20480, NT, GH, GDK)
    z_in = c.sem("w_z_in")
    load_all(c, [(w_z[:, :, :], d["w_z"], z_in)])

    def z_out(act, t, ps):
        nc.scalar.activation(z[:, t], ps[:, 0:BANK].rearrange("p (h n) -> p h n", h=GH), ACT.Silu)
        return nc.scalar.activation(k.ba[:, t, :], ps[:, BANK:520], ACT.Identity)

    token_rows(c, k, "z", hT, w_z, z_in, 520, z_out)
    store_rows(c, "h", [(hT_dram[:, q, :], hT[:, q, :]) for q in range(KD)])
    delta_gates(c, k, k.ba)
    sq = c.area("unit_sq", M + 12288, 2, SEQ)
    root = c.area("unit_root", M + 14336, 2, SEQ)
    unit_rows(c, k, feat, 8, sq, root)
    ktok = c.area("k_tok", M + 12288, NT, GH, GDK)
    vtok = c.area("v_tok", M + 16384, NT, GH, GDK)
    groups = [([feat[:, f + h, P * t:P * t + P] for h in range(GH)], dst[:, t].rearrange("p h n -> p (h n)"), None, None)
              for f, dst in ((4, ktok), (8, vtok)) for t in range(NT)]
    transpose_groups(c, "turn_kv", groups, k.ident)
    kb = c.area("kb_tok", M + 24576, NT, GH, GDK)
    kbT = c.area("kbT", M + 8192, GH, SEQ)
    delta_rows(c, k, ktok, kb, vtok)
    groups = [([kb[:, t, h, :] for t in g4(t0)], kbT[:, h, P * t0:P * t0 + BANK], None, None) for t0 in (0, 4) for h in range(GH)]
    transpose_groups(c, "turn_kb2", groups, k.ident)
    delta_rows2(c, k, ktok, kb)
    PT = c.area("PT", A, NT, GH, P)
    w = (c.area("inv_gtri", A + 4096, 2, BANK), c.area("inv_E", M + 28672, 2, BANK), c.area("inv_LT", M + 29696, 2, BANK),
         c.area("inv_Lm", M + 30720, 2, 6, BANK), c.area("inv_U", A + 5120, 2, BANK), c.area("inv_X", A + 6144, 2, BANK),
         c.area("inv_T", A + 7168, 2, BANK))
    qT, kT = feat[:, 0:4, :], feat[:, 4:8, :]
    delta_inverse(c, k, qT, kT, kbT, kb, vtok, PT, vtok, kb, w)
    W = M + 28672
    o = c.area("delta_out", W + 2048, NT, GH, P)
    delta_scan(c, k, qT, ktok, PT, vtok, kb, c.area("state", W, BANK), c.area("state_decayed", W + 512, BANK),
               c.area("scan_u", W + 1024, BANK), o, c.area("scan_q", W + 1536, BANK))
    k.dbg_o = o
    gated_norm(c, k, o, z, c.area("gnorm_tmp", W, 2, BANK), k.cols)
    k.oaT = c.area("oaT", c.words - 4096, 4, SEQ)
    groups = [([o[:, t, h, :] for t in g4(t0)], k.oaT[:, h, P * t0:P * t0 + BANK], None, None) for t0 in (0, 4) for h in range(GH)]
    transpose_groups(c, "turn_oa", groups, k.ident)
    c.recycle()
    if LAST <= 3: return

    h_in = [c.sem("h_again"), c.sem("w_v_in"), c.sem("bias_in")]
    qkT = c.area("band_qkT", M, 8, SEQ)
    w_v = c.area("w_v", M + 8192, KD, 512)
    v = c.area("band_v", M + 12288, NT, 512)
    bias = c.area("band_bias", M + 16384, HS, 5 * P)
    ring = c.area("band_ring", M + 21504, 4, KD, P)
    load_all(c, [(hT[:, :, :], hT_dram, h_in[0]), (w_v[:, :, :], d["w_vb"], h_in[1]), (bias[:, :, :], d["bias"], h_in[2])])
    with nc.Block(no_gpsimd_drain=True) as block:
        @block.tensor
        def _(pe):
            pe.wait_ge(h_in[0], 16)
    feature_rows(c, k, "band_feat", ring, d["w_qkb"], 8, hT, qkT[:, :, :], None, None, k.qb_scale)
    token_rows(c, k, "band_v", hT, w_v, h_in[1], 512, lambda act, t, ps: nc.scalar.activation(v[:, t, :], ps, ACT.Identity))
    ob = c.area("band_out", M + 21504, NT, 512)
    prob = (c.area("band_prob", M + 8192, 2, 5 * P), c.area("band_probT", M + 9472, 2, 5 * P), c.area("band_cols", M + 10752, 8, 4))
    pre = c.area("band_pre", M + 10784, 2, 5 * P)
    units = []
    for h in range(HS):
        rows = slice(64 * (h % 2), 64 * (h % 2) + 64)
        for qt in range(NT):
            lo = max(qt - 4, 0)
            n = qt - lo + 1
            keys = [(a, qkT[rows, 4 + h // 2, P * lo + a:P * lo + min(a + BANK, P * n)]) for a in range(0, P * n, BANK)]
            units.append(Unit(qkT[rows, h // 2, P * qt:P * qt + P], keys, [v[:, t, 64 * h:64 * h + 64] for t in range(lo, qt + 1)],
                              ob[:, qt, 64 * h:64 * h + 64], bias=((h_in[2], 16) if not units else None, bias[:, h, P * (5 - n):5 * P])))
    attend(c, k, "band", units, 3, 2, prob, pre=pre)
    k.dbg_ob = ob
    obT = c.area("obT", c.words - 8192, 4, SEQ)
    groups = [([ob[:, t, P * q:P * q + P] for t in g4(t0)], obT[:, q, P * t0:P * t0 + BANK], None, None) for t0 in (0, 4) for q in range(4)]
    transpose_groups(c, "turn_ob", groups, k.ident)

    w_ga, w_gb = c.area("w_ga", M, KD, D), c.area("w_gb", M + 8192, KD, D)
    w_a, w_b = c.area("w_a", M + 16384, 4, D), c.area("w_b", M + 20480, 4, D)
    k.branch_in = [c.sem(f"branch_w_in{i}") for i in range(4)]
    k.branch_loads = [(t[:, :, :], d[n], s) for t, n, s in zip((w_ga, w_gb, w_a, w_b), ("w_ga", "w_gb", "w_a", "w_b"), k.branch_in)]
    mix_branches(c, k, d, hT, k.oaT, obT, (w_ga, w_gb), w_a, w_b, c.area("sigmoids", M + 24576, 2, D))
    mixT = c.area("mixT", M + 8192, KD, SEQ)
    groups = [([hT[:, q, P * t:P * t + P] for t in g4(t0)], mixT[:, q, P * t0:P * t0 + BANK], None, None) for t0 in (0, 4) for q in range(KD)]
    transpose_groups(c, "turn_mix", groups, k.ident)
    w_o, x = c.area("w_out_2", M, KD, D), c.area("x_2", M + 16384, NT, D)
    o_in = c.sem("w_out_2_in")

    def out_loads(sp):
        sp.dma_start(w_o[:, :, :], d["w_out_2"]).then_inc(o_in, 16)
        for t in range(NT):
            sp.dma_start(x[:, t, :], k.x_dram[P * t:P * t + P, :]).then_inc(k.tile_in[t], 16)

    mix_out(c, k, "mix_2", mixT, w_o, o_in, None, 4, x, x, before=out_loads)
    k.x3 = x
    if LAST <= 4: return

    store_rows(c, "x3", [(k.x_dram[P * t:P * t + P, :], x[:, t, :]) for t in range(NT)])
    k.junk = c.area("junk3", M, D)
    norm_tokens(c, "norm_3", x, x, NT, k.eps, k.junk, k.stat)
    groups = [([x[:, t, P * q:P * q + P] for t in g4(t0)], hT[:, q, P * t0:P * t0 + BANK], k.norm_ffn2[:, q:q + 1], None)
              for t0 in (0, 4) for q in range(KD)]
    transpose_groups(c, "turn_h4", groups, k.ident)
    actT = c.area("actT", c.words - NF2 * SEQ, NF2, SEQ)
    ring = c.area("ffn_ring", M, 2, 2 * KD, P)
    acc = c.area("ffn_acc", M + 4096, 2, 2, SEQ)
    ffn_up(c, k, d, hT, ring, actT[:, :, :], acc)
    k.turn_down = 5
    x = c.area("x_3", A, NT, D)
    k.norm_rows2 = c.area("norm_rows2", M + 4096, D)
    k.junk = c.area("junk4", M + 5120, D)
    ffn_down(c, k, d, actT, c.area("down_ring", M, 4, 2, BANK), x)
    norm_tokens(c, "norm_4", x, x, NT, k.eps, k.junk, k.stat)
    scale_rows(c, k, x, NT, k.norm_rows2, k.norm_rows_in, 32)
    store_rows(c, "result", [(out[0, P * t:P * t + P, :], x[:, t, :]) for t in range(NT)])


def layout_second(x, a):
    a = {n[:-2]: v for n, v in a.items() if n.endswith("_2")}
    w = a["w_in"][0]
    x["w_feat"] = slices(w[:, 0:1536], P)
    x["w_z"] = by_rows(w[:, 1536:2056])
    x["w_qkb"] = slices(w[:, 2056:3080], P)
    x["w_vb"] = by_rows(w[:, 3080:3592])
    x["w_ga"], x["w_gb"] = by_rows(w[:, 3592:4616]), by_rows(w[:, 4616:5640])
    x["conv_taps"] = np.ascontiguousarray(a["conv_qkv_w"][0].T.reshape(12, P, 4).transpose(1, 0, 2).reshape(P, 48))
    x["dt_bias"], x["a_log"], x["gdn_norm"] = rows(a["dt_bias"][0]), rows(a["a_log"][0]), rows(a["gdn_norm_w"][0])
    x["norm_mix"], x["norm_ffn2"] = columns(a["norm_mix_w"][0]), columns(a["norm_ffn_w"][0])
    x["w_a"], x["w_b"], x["w_out_2"] = by_rows(a["w_branch_a"][0]), by_rows(a["w_branch_b"][0]), by_rows(a["w_out"][0])
    up = a["w_up"][0].reshape(KD, P, 2, NF2, P)
    x["w_ffn"] = np.ascontiguousarray(up.transpose(3, 1, 2, 0, 4).reshape(NF2, P, 2 * KD, P))
    taps = np.concatenate([a["conv_ffn_w"][0], a["conv_ffn_b"]], 0).reshape(4, 2, NF2, P)
    x["ffn_taps"] = np.ascontiguousarray(taps.transpose(3, 2, 1, 0).reshape(P, -1))
    x["w_down_2"] = np.ascontiguousarray(a["w_down"][0].reshape(NF2 // 2, 2, P, 2, BANK).transpose(3, 0, 2, 1, 4))
    x["norm_final_2"] = rows(a["norm_final_w"])
    x["qb_scale"] = np.ascontiguousarray(np.broadcast_to(np.array([DS ** -0.5] * 4 + [1.0] * 4, np.float32), (P, 8)))
    r, j = np.arange(P)[:, None], np.arange(5 * P)[None, :]
    bias = a["rel_bias"][0][:, np.clip(LEAD + r - j, -128, 128) + 128]
    seen = np.where(r < CHUNK, j < LEAD + CHUNK, j >= CHUNK)
    x["bias"] = np.ascontiguousarray(np.where(seen[None], bias, np.float32(NEG)).transpose(1, 0, 2))
    i, o = np.arange(P)[:, None], np.arange(P)[None, :]
    same = i // CHUNK == o // CHUNK
    x["tri"] = (same & (i <= o)).astype(np.float32)
    x["same"] = same.astype(np.float32)
    x["first_half"] = np.broadcast_to(i < CHUNK, (P, P)).astype(np.float32)
    x["second_half"] = np.broadcast_to(i >= CHUNK, (P, P)).astype(np.float32)
    x["mask_up"] = np.tile(np.where(same & (o >= i), 0.0, NEG), (1, GH)).astype("bfloat16")
    lv = [((i >> l) + 1 == (o >> l)) & ((i >> l) % 2 == 0) for l in range(6)]
    x["level"] = np.ascontiguousarray(np.stack(lv, 1).astype(np.float32))


def constants(c, k, d):
    at = [0]

    def put(name, *shape, dtype=F32, parts=P):
        n = int(np.prod(shape)) * (2 if dtype == BF16 else 4) // 4
        t = c.area(name, at[0], *shape, dtype=dtype, parts=parts)
        at[0] += -(-n // 8) * 8
        return t

    k.constants = []
    k.eps, k.stat, k.tmp = put("eps", 1), put("stat", 3, NK), put("tmp", D)
    def loaded(name, *shape, dtype=F32):
        t = put(name, *shape, dtype=dtype)
        k.constants.append((t[:], d[name]))
        return t

    k.ident, k.ident_bf = loaded("ident", P), loaded("ident_bf", P, dtype=BF16)
    k.F2 = at[0]
    k.mask_prev, k.mask_next = loaded("mask_prev", P, dtype=BF16), loaded("mask_next", P, dtype=BF16)
    k.rope_a, k.rope_b = loaded("rope_a", NT, 2, DA), loaded("rope_b", NT, 2, ROPE)
    k.b_mod, k.norm_attn, k.norm_ffn = loaded("b_mod", 32), loaded("norm_attn", KD), loaded("norm_ffn", KD)
    k.q_norm, k.kv_norm, k.sink = loaded("q_norm", KQ), loaded("kv_norm", KKV), loaded("sink", HA)
    k.gate_a, k.gate_f = loaded("gate_a", D), loaded("gate_f", D)
    k.const_in = c.sem("constants_in")
    k.cond = put("cond", KD, 2)
    k.silu_c = put("silu_c", KD, 2)
    k.silu_rows = put("silu_rows", KD, P)
    k.mod = put("mod", 32, 2)
    k.scale_a, k.scale_ac, k.scale_f = put("scale_a", KD), put("scale_ac", KD), put("scale_f", KD)
    k.F = at[0]


class Kept:
    pass


LAST = 99


def program(nc, d, out):
    c, k = Core(nc), Kept()
    constants(c, k, d)
    mod_vectors(c, k, d)
    first_attention(c, k, d)
    c.recycle()
    if LAST <= 1: return c, k
    first_experts(c, k, d)
    c.recycle()
    if LAST <= 2: return c, k
    second_block(c, k, d, out)
    return c, k


def rope_tables(dim, heads_first=False):
    nf = dim // 4
    pos = np.arange(SEQ)
    inv = np.float32(10000.0) ** (-np.arange(nf, dtype=np.float32) / nf)
    table = np.zeros((SEQ, 2, 2, 2, nf), np.float32)
    for a, p in enumerate((pos // 64, pos % 64)):
        ang = p.astype(np.float32)[:, None] * inv[None, :]
        table[:, 0, a, 0] = table[:, 0, a, 1] = np.cos(ang)
        table[:, 1, a, 0], table[:, 1, a, 1] = -np.sin(ang), np.sin(ang)
    return np.ascontiguousarray(table.reshape(NT, P, 2, dim).transpose(1, 0, 2, 3))


def columns(v):
    return np.ascontiguousarray(v.reshape(-1, P).T)


def by_rows(w):
    return np.ascontiguousarray(w.reshape(-1, P, w.shape[-1]).transpose(1, 0, 2))


def slices(w, n):
    return np.ascontiguousarray(w.reshape(w.shape[0] // P, P, -1, n).transpose(2, 1, 0, 3))


def rows(v):
    return np.ascontiguousarray(np.broadcast_to(v.reshape(1, -1), (P, v.size)))


def layout(i):
    a = {n: np.asarray(v) for n, v in i.items()}
    x = {}
    x["x"], x["ctx"] = a["x"], a["ctx"]
    x["cond"] = np.ascontiguousarray(np.stack([a["c"].reshape(KD, P).T, a["c_ctx"].reshape(KD, P).T], -1))
    order = [0, 1, 3, 4, 2, 5]
    wm = a["w_mod"][0].reshape(D, 6, D)[:, order].reshape(D, 6 * D)
    x["w_mod"] = slices(wm, 512)
    bm = a["b_mod"][0].reshape(6, D)[order]
    x["b_mod"] = columns(bm[:4].reshape(-1))
    x["gate_a"], x["gate_f"] = rows(bm[4]), rows(bm[5])
    x["norm_attn"], x["norm_ffn"] = columns(a["norm_attn"][0]), columns(a["norm_ffn"][0])
    x["q_norm"], x["kv_norm"] = columns(a["q_norm"][0]), columns(a["kv_norm"][0])
    x["sink"] = rows(a["sink"][0])
    x["ident"] = np.eye(P, dtype=np.float32)
    x["ident_bf"] = np.eye(P).astype("bfloat16")
    i0, j0 = np.arange(P)[:, None], np.arange(P)[None, :]
    x["mask_prev"] = np.where(j0 < i0, NEG, 0.0).astype("bfloat16")
    x["mask_next"] = np.where(j0 > i0, NEG, 0.0).astype("bfloat16")
    x["rope_a"], x["rope_b"] = rope_tables(64), rope_tables(32)
    w = a["w_in"][0]
    q = w[:, 0:512].reshape(D, 2, 4, 64).transpose(0, 2, 1, 3).reshape(D, 512)
    x["w_in"] = by_rows(np.concatenate([q, w[:, 512:640], w[:, 640:768], w[:, 1152:1408], w[:, 1408:1440], w[:, 768:1152]], 1))
    x["w_q_up"] = by_rows(a["w_q_up"][0])
    kv = a["w_kv_up"][0].reshape(KVR, HB, 2, 64)
    x["w_kv_up"] = by_rows(np.concatenate([kv[:, :, 0].reshape(KVR, 512), kv[:, :, 1].reshape(KVR, 512)], 1))
    x["w_out"] = by_rows(a["w_out"][0])
    if LAST > 1:
        layout_experts(x, a)
    if LAST > 2:
        layout_second(x, a)
    return x


def kernel(**inputs):
    import concourse.bacc as bacc
    from concourse.bass_utils import run_bass_kernel_spmd

    nc = bacc.Bacc("TRN2", target_bir_lowering=False, num_devices=1)
    arrays, d = {}, {}
    for name, v in layout(inputs).items():
        arrays[f"in_{name}"] = v
        d[name] = nc.dram_tensor(f"in_{name}", v.shape, mybir.dt.from_np(v.dtype), kind="ExternalInput").ap()
    out = nc.dram_tensor("out", (1, SEQ, D), F32, kind="ExternalOutput").ap()
    program(nc, d, out)
    return run_bass_kernel_spmd(nc, [arrays], core_ids=[0]).results[0]["out"]
```
